# Optimizing a Trainium2 kernel written in Bass

```python
import math
import jax, jax.numpy as jnp
from jax import lax
import numpy as np

D_MODEL = 2048
BATCH = 1
SEQ = 256
DEPTH = 1

N_HEADS = 8
HEAD_DIM = 128
ATTN_DIM = N_HEADS * HEAD_DIM
IDX_HEADS = 16
IDX_DIM = 64
TOPK_MAX = 256
Q_BLOCK = 128
NUM_BUCKETS = 32
MAX_DISTANCE = 128
CONV_CH = 1024
CONV_WIDTH = 31
D_FF = 5632
FFN_RES_WEIGHT = 0.5
EPS = 1e-6

IN_SPLITS = (ATTN_DIM,
             ATTN_DIM,
             ATTN_DIM,
             IDX_HEADS * IDX_DIM,
             IDX_DIM,
             IDX_HEADS,
             2 * CONV_CH,
             2 * D_MODEL)
IN_DIM = int(sum(IN_SPLITS))
IN_OFFSETS = tuple(int(o) for o in np.cumsum(IN_SPLITS)[:-1])

kernel_name = "hybrid_dsa_conformer_gated_macaron"

def rmsnorm(x, g):
    xf = x.astype(jnp.float32)
    y = xf * lax.rsqrt(jnp.mean(xf * xf, axis=-1, keepdims=True) + EPS)
    return (y * g.astype(jnp.float32)).astype(x.dtype)

def layernorm(x, g, b):
    xf = x.astype(jnp.float32)
    mu = jnp.mean(xf, axis=-1, keepdims=True)
    var = jnp.mean(jnp.square(xf - mu), axis=-1, keepdims=True)
    y = (xf - mu) * lax.rsqrt(var + EPS)
    return (y * g.astype(jnp.float32) + b.astype(jnp.float32)).astype(x.dtype)

def swiglu(x, wg, wu, wd):
    return (jax.nn.silu(x @ wg) * (x @ wu)) @ wd

def t5_bucket(dist):
    max_exact = NUM_BUCKETS // 2
    n = jnp.maximum(dist, 0)
    nf = jnp.maximum(n, max_exact).astype(jnp.float32)
    large = max_exact + (jnp.log(nf / max_exact) / math.log(MAX_DISTANCE / max_exact)
                         * (NUM_BUCKETS - max_exact)).astype(jnp.int32)
    large = jnp.minimum(large, NUM_BUCKETS - 1)
    return jnp.where(n < max_exact, n, large)

def dsa_attention(q, k, v, q_idx, k_idx, w_idx, rel_bias):
    B, S = q.shape[0], q.shape[1]
    topk = min(TOPK_MAX, S // 4)
    nb = S // Q_BLOCK
    s_pos = jnp.arange(S, dtype=jnp.int32)
    k_idx_f = k_idx.astype(jnp.float32)
    bias_tab = rel_bias.astype(jnp.float32)
    scale = HEAD_DIM ** -0.5

    def to_blocks(a):
        return jnp.moveaxis(a.reshape((B, nb, Q_BLOCK) + a.shape[2:]), 1, 0)

    def block_fn(args):
        qb, qib, wb, t0 = args
        t_pos = t0 + jnp.arange(Q_BLOCK, dtype=jnp.int32)
        dots = jnp.einsum('bthd,bsd->bths', qib.astype(jnp.float32), k_idx_f) * (IDX_DIM ** -0.5)
        score = jnp.einsum('bths,bth->bts', jax.nn.relu(dots), wb.astype(jnp.float32))
        causal = s_pos[None, :] <= t_pos[:, None]
        score = jnp.where(causal[None], score, -jnp.inf)
        _, sel = lax.top_k(score, topk)
        valid = sel <= t_pos[None, :, None]
        k_sel = jax.vmap(lambda kk, ii: kk[ii])(k, sel)
        v_sel = jax.vmap(lambda vv, ii: vv[ii])(v, sel)
        logits = jnp.einsum('bthd,btkhd->bthk', qb.astype(jnp.float32),
                            k_sel.astype(jnp.float32)) * scale
        bias = bias_tab[t5_bucket(t_pos[None, :, None] - sel)]
        logits = logits + jnp.moveaxis(bias, 3, 2)
        logits = jnp.where(valid[:, :, None, :], logits, -jnp.inf)
        p = jax.nn.softmax(logits, axis=-1)
        out = jnp.einsum('bthk,btkhd->bthd', p, v_sel.astype(jnp.float32))
        return out.astype(v.dtype)

    starts = jnp.arange(nb, dtype=jnp.int32) * Q_BLOCK
    out = lax.map(block_fn, (to_blocks(q), to_blocks(q_idx), to_blocks(w_idx), starts))
    return jnp.moveaxis(out, 0, 1).reshape(B, S, ATTN_DIM)

def conv_module(glu_in, dw, dw_b, ln_g, ln_b, w_pw2):
    a, gate = jnp.split(glu_in, 2, axis=-1)
    h = a * jax.nn.sigmoid(gate)
    h = lax.conv_general_dilated(h, dw[:, None, :].astype(h.dtype), window_strides=(1,),
                                 padding=[(CONV_WIDTH - 1, 0)],
                                 dimension_numbers=('NWC', 'WIO', 'NWC'),
                                 feature_group_count=CONV_CH) + dw_b
    h = jax.nn.silu(layernorm(h, ln_g, ln_b))
    return h @ w_pw2

def setup_inputs(seed: int = 0) -> dict:
    key = jax.random.key(seed)
    ks = iter(jax.random.split(key, 32))
    f32 = jnp.float32

    def w(shape, fan_in):
        return jax.random.normal(next(ks), (DEPTH,) + shape, f32) * fan_in ** -0.5

    def gain(n):
        return 1.0 + 0.05 * jax.random.normal(next(ks), (DEPTH, n), f32)

    def small(n, s=0.02):
        return s * jax.random.normal(next(ks), (DEPTH, n), f32)

    x = jax.random.normal(next(ks), (BATCH, SEQ, D_MODEL), f32)
    rel_bias = 0.5 * jax.random.normal(next(ks), (NUM_BUCKETS, N_HEADS), f32)
    return {
        "x": x,
        "rel_bias": rel_bias,
        "ffn1_pre_g": gain(D_MODEL),
        "ffn1_wg": w((D_MODEL, D_FF), D_MODEL),
        "ffn1_wu": w((D_MODEL, D_FF), D_MODEL),
        "ffn1_wd": w((D_FF, D_MODEL), D_FF),
        "ffn1_post_g": gain(D_MODEL),
        "mix_pre_g": gain(D_MODEL),
        "w_in": w((D_MODEL, IN_DIM), D_MODEL),
        "b_gate": small(2 * D_MODEL, 0.1),
        "w_o": w((ATTN_DIM, D_MODEL), ATTN_DIM),
        "conv_dw": w((CONV_WIDTH, CONV_CH), CONV_WIDTH),
        "conv_dw_b": small(CONV_CH),
        "conv_ln_g": gain(CONV_CH),
        "conv_ln_b": small(CONV_CH),
        "w_pw2": w((CONV_CH, D_MODEL), CONV_CH),
        "w_out": w((D_MODEL, D_MODEL), D_MODEL),
        "mix_post_g": gain(D_MODEL),
        "ffn2_pre_g": gain(D_MODEL),
        "ffn2_wg": w((D_MODEL, D_FF), D_MODEL),
        "ffn2_wu": w((D_MODEL, D_FF), D_MODEL),
        "ffn2_wd": w((D_FF, D_MODEL), D_FF),
        "ffn2_post_g": gain(D_MODEL),
    }

def reference(x, rel_bias, ffn1_pre_g, ffn1_wg, ffn1_wu, ffn1_wd, ffn1_post_g,
              mix_pre_g, w_in, b_gate, w_o, conv_dw, conv_dw_b, conv_ln_g, conv_ln_b,
              w_pw2, w_out, mix_post_g, ffn2_pre_g, ffn2_wg, ffn2_wu, ffn2_wd, ffn2_post_g):
    B, S, _ = x.shape
    h = x
    for l in range(DEPTH):
        f = swiglu(rmsnorm(h, ffn1_pre_g[l]), ffn1_wg[l], ffn1_wu[l], ffn1_wd[l])
        h = h + FFN_RES_WEIGHT * rmsnorm(f, ffn1_post_g[l])

        u = rmsnorm(h, mix_pre_g[l])
        proj = u @ w_in[l]
        q, k, v, qi, ki, wi, glu_in, gates = jnp.split(proj, IN_OFFSETS, axis=-1)
        q = q.reshape(B, S, N_HEADS, HEAD_DIM)
        k = k.reshape(B, S, N_HEADS, HEAD_DIM)
        v = v.reshape(B, S, N_HEADS, HEAD_DIM)
        qi = qi.reshape(B, S, IDX_HEADS, IDX_DIM)
        wi = wi * (IDX_HEADS ** -0.5)
        attn = dsa_attention(q, k, v, qi, ki, wi, rel_bias) @ w_o[l]
        conv = conv_module(glu_in, conv_dw[l], conv_dw_b[l], conv_ln_g[l],
                           conv_ln_b[l], w_pw2[l])
        g_attn, g_conv = jnp.split(jax.nn.sigmoid(gates + b_gate[l]), 2, axis=-1)
        mixed = (g_attn * attn + g_conv * conv) @ w_out[l]
        h = h + rmsnorm(mixed, mix_post_g[l])

        f = swiglu(rmsnorm(h, ffn2_pre_g[l]), ffn2_wg[l], ffn2_wu[l], ffn2_wd[l])
        h = h + FFN_RES_WEIGHT * rmsnorm(f, ffn2_post_g[l])
    return h


_drawn_inputs = setup_inputs


def setup_inputs(seed=0):
    import zlib

    import numpy as np

    out = dict(_drawn_inputs(seed))
    spreads = {}
    factors = {'conv_ln_b': 4.273, 'ffn2_post_g': 3.581}
    for name, (base, spread) in spreads.items():
        noise = np.random.default_rng([zlib.crc32(name.encode()), seed]).standard_normal(out[name].shape)
        drawn = base * np.exp(spread * noise) if base else spread * noise
        out[name] = __import__('jax').numpy.asarray(drawn.astype(out[name].dtype))
    for name, factor in factors.items():
        out[name] = (out[name] * factor).astype(out[name].dtype)
    return out
```

```python
import numpy as np
import concourse.bass as bass
from concourse import mybir
from contextlib import ExitStack

P = 128
D = 2048
SEQ = 256
TT = SEQ // P
KT = D // P
FF = 5632
FT = FF // P
CW = 512
EPS = 1e-6
HEADS, HD = 8, 128
IH, IDIM = 16, 64
CONV = 1024
CT = CONV // P
TAPS = 31
PAD = TAPS - 1
TOPK = 64
BUCKETS = 32
RING = 4
SK = 2
BLK = D // CW
KB = CW // P
MASKED = -1.0e30
TAKEN = -3.0e30
SPAN = 2 * P + P
RELS = 3 * P - 1
Q_AT, K_AT, V_AT, QI_AT = 0, 1024, 2048, 3072
KI_AT = 4096
GLU_AT = KI_AT + IDIM + IH
GATE_AT = GLU_AT + 2 * CONV
NSMALL = IDIM + IH

UP_CHUNKS = FF // CW
UP_SLABS = 2 * KT // SK
DOWN_SLABS = FT // SK
FFN_LEFT = UP_CHUNKS + BLK // 2
FFN_SLABS = UP_CHUNKS * UP_SLABS + BLK * DOWN_SLABS


def mix_chunks():
    plan = [("a0", 8, 0), ("gt0", 8, 1), ("a1", 8, 0), ("gt1", 8, 1), ("kiwi", 4, 0)]
    plan += [(f"qk{i}", 8, 1 - i % 2) for i in range(6)]
    plan += [(f"v{i}", 8, 1 - i) for i in range(2)]
    plan += [(f"gc{i}", 8, 1 - i % 2) for i in range(BLK)]
    plan += [(f"pw{i}", 4, 1 - i % 2) for i in range(BLK)]
    for i in range(BLK):
        plan += [(f"ga{i}", 8, 1), (f"wo{i}", 4, 0)]
    plan += [(f"out{i}", 8, 1 - i % 2) for i in range(BLK)]
    at, freed, table = FFN_SLABS, [FFN_LEFT, FFN_LEFT], {}
    for name, slabs, buf in plan:
        table[name] = (at, slabs, buf, freed[buf])
        at += slabs
        freed[buf] += 1
    return table, at, freed


MIX, MIX_END, MIX_FREED = mix_chunks()


def build(nc, x, rel_bias, f1_pre, f1_wg, f1_wu, f1_wd, f1_post, mix_pre, w_in, b_gate, w_o, conv_dw,
          conv_dw_b, ln_g, ln_b, w_pw2, w_out, mix_post, f2_pre, f2_wg, f2_wu, f2_wd, f2_post,
          bucket_rows, bias_scratch, out):
    f32, f32r = mybir.dt.float32, mybir.dt.float32r
    ALU, ACT, AX = mybir.AluOpType, mybir.ActivationFunctionType, mybir.AxisListType

    ctx = ExitStack()
    with ctx:
        at = [nc.sbuf_base + (-nc.sbuf_base) % 64]

        def sb(name, shape, dt=f32, over=None):
            size = 4 * int(np.prod(shape[1:]))
            size += -size % 32
            off = at[0] if over is None else over
            if over is None:
                at[0] += size
            return nc.alloc_sbuf_tensor_at(name, shape, dt, offset=off), off

        res, _ = sb("res", [P, TT, D])
        act_hi, o_act = sb("act_hi", [P, KT, SEQ], f32r)
        act_lo, _ = sb("act_lo", [P, KT, SEQ], f32r)
        fout, _ = sb("fout", [P, BLK, TT, CW], over=o_act)
        raw, _ = sb("raw", [P, RING, SK * CW])
        whi, _ = sb("whi", [P, RING, SK * CW], f32r)
        wlo, _ = sb("wlo", [P, RING, SK * CW], f32r)
        h_hi, o_h = sb("h_hi", [P, FT, SEQ], f32r)
        h_lo, _ = sb("h_lo", [P, FT, SEQ], f32r)
        h_end = at[0]
        gpost, o_gpost = sb("gpost", [P, D])
        sg, o_sg = sb("sg", [P, TT, CW])
        nat, _ = sb("nat", [P, TT, CW])
        junk, _ = sb("junk", [P, D], over=o_sg)
        vrows, _ = sb("vrows", [P, P], over=o_sg)
        bgate, _ = sb("bgate", [P, 2, CW])
        minus_half, _ = sb("minus_half", [P, 1])
        ident, _ = sb("ident", [P, P])
        mean_w, _ = sb("mean_w", [P, P])
        vec, _ = sb("vec", [P, 80])
        small, _ = sb("small", [P, TT, NSMALL])
        fsq, _ = sb("fsq", [P, TT, BLK])
        stat, _ = sb("stat", [P, 56])
        dwt, _ = sb("dwt", [P, CT, TAPS])
        assert at[0] <= nc.sbuf_usable_end, at[0]

        at[0] = o_h
        conv_in, o_cin = sb("conv_in", [P, CT, PAD + SEQ])
        conv_out, o_cout = sb("conv_out", [P, CT, SEQ])
        qi_t, o_qi = sb("qi_t", [P, IH // 2, SEQ])
        ki_t, _ = sb("ki_t", [P, 2, SEQ])
        q_t, o_q = sb("q_t", [P, HEADS, SEQ])
        k_t, _ = sb("k_t", [P, HEADS, SEQ])
        v_n, _ = sb("v_n", [P, TT, HEADS * HD])
        bias, _ = sb("bias", [P, HEADS, SPAN])
        gconv, o_gconv = sb("gconv", [P, BLK, TT, CW])
        score, o_score = sb("score", [P, SPAN])
        work, o_work = sb("work", [P, SPAN])
        addmask, _ = sb("addmask", [P, SPAN])
        p_t, o_pt = sb("p_t", [P, 2, SPAN])
        rel_rows, _ = sb("rel_rows", [HEADS, RELS])
        assert at[0] <= h_end, at[0]
        squares, _ = sb("squares", [P, CT, SEQ], over=o_cin)
        conv_hi, _ = sb("conv_hi", [P, CT, SEQ], f32r, over=o_cin)
        conv_lo, _ = sb("conv_lo", [P, CT, SEQ], f32r, over=o_cout)
        attn_hi, _ = sb("attn_hi", [P, HEADS, SEQ], f32r, over=o_qi)
        attn_lo, _ = sb("attn_lo", [P, HEADS, SEQ], f32r, over=o_gpost)
        mix_hi, _ = sb("mix_hi", [P, KT, SEQ], f32r, over=o_q)
        mix_lo, _ = sb("mix_lo", [P, KT, SEQ], f32r, over=o_q + KT * SEQ * 4)
        relu_d, _ = sb("relu_d", [P, 2, 2 * SEQ], over=o_sg)
        logit = [sb("logit0", [P, SPAN], over=o_score)[0], sb("logit1", [P, SPAN], over=o_work)[0]]
        ln_rstd, _ = sb("ln_rstd", [P, 1, SEQ], over=o_pt)
        ki_pad, _ = sb("ki_pad", [P, TT, 2, P], over=o_pt)
        dw_rows, _ = sb("dw_rows", [TAPS, CONV], over=o_gconv)
        onehot, _ = sb("onehot", [BUCKETS, RELS + 1], over=o_gconv + 4096)
        relb, _ = sb("relb", [BUCKETS, HEADS], over=o_gconv + 4096 + 4 * (RELS + 1))

        acc = ctx.enter_context(nc.psum_tensor("acc", [P, 2, TT, CW], f32))
        msc = ctx.enter_context(nc.psum_tensor("msc", [P, 4, CW], f32))
        blocks = msc[:].rearrange("p b (c t) -> p (b c) t", t=SEQ)

        def sem(name):
            return ctx.enter_context(nc.semaphore(name))

        raw_full = [sem(f"raw_full{i}") for i in range(RING)]
        hi_ready, lo_ready, mm_done = sem("hi_ready"), sem("lo_ready"), sem("mm_done")
        acc_free = [sem("acc_free0"), sem("acc_free1")]
        x_full = [sem(f"x_full{b}") for b in range(BLK)]
        consts_ready, vec_loaded, vec_psum, vec_ready = sem("consts_ready"), sem("vec_loaded"), sem("vec_psum"), sem("vec_ready")
        res_ready, act_psum, acthi_ready, actlo_ready = sem("res_ready"), sem("act_psum"), sem("acthi_ready"), sem("actlo_ready")
        squared = sem("squared")
        ssq_ready, root_asked, root_ready = sem("ssq_ready"), sem("root_asked"), sem("root_ready")
        h_psum, hhi_ready, hlo_ready = sem("h_psum"), sem("hhi_ready"), sem("hlo_ready")
        gpost_full = sem("gpost_full")
        stored = sem("stored")
        dve_step = sem("dve_step")
        zeros_ready, mixrows_full = sem("zeros_ready"), sem("mixrows_full")
        tr_psum, tr_evicted = sem("tr_psum"), sem("tr_evicted")
        glu_ready = sem("glu_ready")
        bias_out, bias_full = sem("bias_out"), sem("bias_full")
        conv_tap = sem("conv_tap")
        ln_psum, ln_centred, ln_squares, ln_scaled, convf_ready, convhi_ready, convlo_ready = (
            sem("ln_psum"), sem("ln_centred"), sem("ln_squares"), sem("ln_scaled"), sem("convf_ready"),
            sem("convhi_ready"), sem("convlo_ready"))
        ln_var, ln_std = sem("ln_var"), sem("ln_std")
        dots_ready, relu_ready, score_added, score_masked, sel_ready, mask_ready = (
            sem("dots_ready"), sem("relu_ready"), sem("score_added"), sem("score_masked"),
            sem("sel_ready"), sem("mask_ready"))
        logit_psum, max_ready, exp_ready, prob_ready, pt_psum, pt_ready, pv_psum, athi_ready, atlo_ready = (
            sem("logit_psum"), sem("max_ready"), sem("exp_ready"), sem("prob_ready"), sem("pt_psum"),
            sem("pt_ready"), sem("pv_psum"), sem("athi_ready"), sem("atlo_ready"))
        bgate_full, gate_ready = [sem("bgate_full0"), sem("bgate_full1")], sem("gate_ready")
        mixed_ready, mixed_psum, mixhi_ready, mixlo_ready = sem("mixed_ready"), sem("mixed_psum"), sem("mixhi_ready"), sem("mixlo_ready")

        ROOT_OF_PHASE = [1, 3, 5]
        PRE = [0, KT, 2 * KT]
        DWB, LNG, LNB = 3 * KT, 3 * KT + CT, 3 * KT + 2 * CT
        NVEC = 3 * KT + 3 * CT
        RSTD, RPOST, TMP, MX, NMX, RSUM, RINV, MAX8 = 0, 2, 4, 8, 12, 16, 20, 32

        ffn_base = [0, MIX_END]
        freed0 = [[0, 0], MIX_FREED]
        w_up = [(f1_wg, f1_wu), (f2_wg, f2_wu)]
        w_down = [f1_wd, f2_wd]

        def rows(w):
            return w.rearrange("(k p) n -> p k n", p=P)

        def slot_view(t, slot, kts, width):
            return t[:, slot, 0:kts * width].rearrange("p (k n) -> p k n", n=width)

        block = ctx.enter_context(nc.Block())

        @block.sync
        def _(sp):
            def load(n, j, src, slabs_done, kts=SK, width=CW, wait=True):
                if wait:
                    sp.wait_ge(lo_ready, slabs_done)
                sp.dma_start(slot_view(raw, j % RING, kts, width), src).then_inc(raw_full[j % RING], 16)

            xv = x.rearrange("(t p) n -> p t n", p=P)
            for b in range(BLK):
                sp.dma_start(res[:, :, b * CW:(b + 1) * CW], xv[:, :, b * CW:(b + 1) * CW]).then_inc(x_full[b], 16)

            def ffn(f):
                base = ffn_base[f]

                def up(it):
                    for j in range(UP_SLABS):
                        w, k = rows(w_up[f][j // (UP_SLABS // 2)]), (j % (UP_SLABS // 2)) * SK
                        load(None, j, w[:, k:k + SK, bass.ts(it, CW)], base + UP_SLABS * it + j - RING + 1,
                             wait=not (f == 0 and isinstance(it, int) and j < RING))

                up(0)
                with sp.Fori(1, UP_CHUNKS) as it:
                    up(it)
                down0 = base + UP_CHUNKS * UP_SLABS
                with sp.Fori(0, BLK // 2) as i:
                    for j in range(2 * DOWN_SLABS):
                        half, k = j // DOWN_SLABS, (j % DOWN_SLABS) * SK
                        load(None, j, rows(w_down[f])[:, k:k + SK, bass.ds(i * (2 * CW) + half * CW, CW)],
                             down0 + 2 * DOWN_SLABS * i + j - RING + 1)

            def chunk(name, w, col, width=CW, kts=SK):
                n0, slabs, _, _ = MIX[name]
                for j in range(slabs):
                    load(n0 + j, j, rows(w)[:, j * kts:(j + 1) * kts, col:col + width], n0 + j - RING + 1, kts, width)

            ffn(0)
            for i in range(2):
                chunk(f"a{i}", w_in, GLU_AT + i * CW)
                chunk(f"gt{i}", w_in, GLU_AT + CONV + i * CW)
            chunk("kiwi", w_in, KI_AT, NSMALL, 4)
            for i, col in enumerate((QI_AT, QI_AT + CW, Q_AT, Q_AT + CW, K_AT, K_AT + CW)):
                chunk(f"qk{i}", w_in, col)
            for i in range(2):
                chunk(f"v{i}", w_in, V_AT + i * CW)
            for i in range(BLK):
                chunk(f"gc{i}", w_in, GATE_AT + D + i * CW)
            for i in range(BLK):
                chunk(f"pw{i}", w_pw2, i * CW)
            for i in range(BLK):
                chunk(f"ga{i}", w_in, GATE_AT + i * CW)
                chunk(f"wo{i}", w_o, i * CW)
            for i in range(BLK):
                chunk(f"out{i}", w_out, i * CW)
            ffn(1)
            ov = out.rearrange("(t p) n -> p t n", p=P)
            for b in range(BLK):
                sp.wait_ge(res_ready, 2 * BLK + b + 1)
                sp.dma_start(ov[:, :, b * CW:(b + 1) * CW], res[:, :, b * CW:(b + 1) * CW]).then_inc(stored, 16)
            sp.wait_ge(stored, 16 * BLK)

        @block.gpsimd
        def _(pool):
            vr = [(f1_pre, KT), (mix_pre, KT), (f2_pre, KT), (conv_dw_b, CT), (ln_g, CT), (ln_b, CT)]
            r = 0
            for v, n in vr:
                pool.dma_start(vrows[r:r + n, :], v.rearrange("(k p) -> k p", p=P)).then_inc(vec_loaded, 16)
                r += n
            nc.gpsimd.memset(ident[:], 0.0).then_inc(zeros_ready, 1)
            nc.gpsimd.memset(mean_w[:], 1.0 / CONV)
            pool.wait_ge(zeros_ready, 1)
            nc.gpsimd.affine_select(out=ident[:], in_=ident[:], compare_op=ALU.not_equal, fill=1.0, base=0,
                                    pattern=[[-1, P]], channel_multiplier=1).then_inc(consts_ready, 1)

            def load_gpost(g, n):
                pool.dma_start(gpost[:], g.rearrange("(o n) -> o n", o=1).to_broadcast([P, D])).then_inc(gpost_full, 16)

            def root(n, t):
                pool.wait_ge(root_asked, n)
                nc.gpsimd.tensor_tensor(t, t, minus_half[:].to_broadcast([P, t.shape[-1]]), ALU.pow).then_inc(root_ready, 1)

            load_gpost(f1_post, 0)
            nc.gpsimd.memset(minus_half[:], -0.5).then_inc(zeros_ready, 1)
            pool.wait_ge(zeros_ready, 2)
            rstd, rpost = stat[:, RSTD:RSTD + 2], stat[:, RPOST:RPOST + 2]
            root(1, rstd)
            root(2, rpost)
            pool.wait_ge(mm_done, FFN_SLABS)
            nc.gpsimd.memset(conv_in[:, :, 0:PAD], 0.0)
            nc.gpsimd.memset(ki_pad[:], 0.0).then_inc(zeros_ready, 1)
            pool.dma_start(dw_rows[:], conv_dw).then_inc(mixrows_full, 16)
            pool.dma_start(onehot[:, 0:RELS], bucket_rows).then_inc(mixrows_full, 16)
            pool.dma_start(relb[:], rel_bias).then_inc(mixrows_full, 16)
            root(3, rstd)
            pool.wait_ge(tr_evicted, 2)
            pool.dma_start(bias_scratch, rel_rows[:].rearrange("h (o r) -> h o r", o=1).to_broadcast([HEADS, P, RELS])).then_inc(bias_out, 16)
            pool.wait_ge(bias_out, 16)
            for h in range(HEADS):
                skew = bass.AP(bias_scratch.tensor, h * P * RELS + P - 1, [[RELS - 1, P], [1, SEQ]])
                pool.dma_start(bias[:, h, 0:SEQ], skew).then_inc(bias_full, 16)
                skew = bass.AP(bias_scratch.tensor, h * P * RELS + 2 * P - 1, [[RELS - 1, P], [1, P]])
                pool.dma_start(bias[:, h, SEQ:SPAN], skew).then_inc(bias_full, 16)

            gates = [f"gc{i}" for i in range(BLK)] + [f"ga{i}" for i in range(BLK)]

            def load_bgate(g):
                col = (D if g < BLK else 0) + (g % BLK) * CW
                if g >= 2:
                    _, _, buf, freed = MIX[gates[g - 2]]
                    pool.wait_ge(acc_free[buf], freed + 1)
                pool.dma_start(bgate[:, g % 2, :], b_gate[col:col + CW].rearrange("(o n) -> o n", o=1)
                               .to_broadcast([P, CW])).then_inc(bgate_full[g % 2], 16)

            load_bgate(0)
            load_bgate(1)
            load_bgate(2)

            def causal(t, fill_value):
                nc.gpsimd.affine_select(out=t[:, 0:SEQ], in_=t[:, 0:SEQ], compare_op=ALU.is_ge, fill=fill_value,
                                        base=P, pattern=[[-1, SEQ]], channel_multiplier=1)
                return nc.gpsimd.affine_select(out=t[:, SEQ:SPAN], in_=t[:, SEQ:SPAN], compare_op=ALU.is_ge,
                                               fill=fill_value, base=0, pattern=[[-1, P]], channel_multiplier=1)

            pool.wait_ge(score_added, 4 * IH // 2 + 1)
            causal(score, MASKED).then_inc(score_masked, 1)
            load_bgate(3)
            pool.wait_ge(sel_ready, 1)
            causal(addmask, MASKED).then_inc(mask_ready, 1)
            for g in range(BLK, 2 * BLK):
                load_bgate(g)
            pool.wait_ge(mm_done, MIX["wo3"][0] + MIX["wo3"][1])
            load_gpost(mix_post, 1)
            root(4, rpost)
            load_gpost(f2_post, 2)
            root(5, rstd)
            root(6, rpost)
            for s in (vec_loaded, 16 * 6), (gpost_full, 48), (bias_full, 32 * HEADS):
                pool.wait_ge(*s)

        @block.scalar
        def _(act):
            def hi(j, done, loads, first=False, kts=SK, width=CW):
                act.wait_ge(raw_full[j % RING], 16 * loads)
                if not first:
                    act.wait_ge(mm_done, done)
                nc.scalar.activation(whi[:, j % RING, 0:kts * width], raw[:, j % RING, 0:kts * width],
                                     ACT.Copy).then_inc(hi_ready, 1)

            def act_hi_block(p, b):
                act.wait_ge(act_psum, BLK * p + b + 1)
                if p == 0 and b == 0:
                    act.wait_ge(vec_ready, 1)
                for k in range(KB):
                    kt = KB * b + k
                    ins = nc.scalar.activation(act_hi[:, kt, :], blocks[:, KB * (b % 2) + k, :], ACT.Copy,
                                               scale=vec[:, PRE[p] + kt:PRE[p] + kt + 1])
                ins.then_inc(acthi_ready, 1)

            def row_squares(p):
                if p == 0:
                    for b in range(BLK):
                        act.wait_ge(x_full[b], 16)
                else:
                    act.wait_ge(res_ready, BLK * p)
                for t in range(TT):
                    if t:
                        act.wait_ge(ssq_ready, TT * p + t)
                    nc.scalar.activation(junk[:], res[:, t, :], ACT.Square,
                                         accum_out=stat[:, TMP + t:TMP + t + 1]).then_inc(ssq_ready, 1)

            def start_phase(p, hi_at):
                for j in range(RING):
                    hi_at(j)
                act_hi_block(p, 0)
                act_hi_block(p, 1)
                hi_at(4)
                hi_at(5)
                act_hi_block(p, 2)
                hi_at(6)
                hi_at(7)
                act_hi_block(p, 3)
                row_squares(p)

            def down_squares(buf, o):
                for t in range(TT):
                    nc.scalar.activation(junk[:, (TT * buf + t) * CW:(TT * buf + t + 1) * CW], acc[:, buf, t, :], ACT.Square, accum_out=fsq[:, t, bass.ds(o, 1)]).then_inc(squared, 1)

            def ffn(f):
                base, p = ffn_base[f], 2 * f

                def up(it, peeled):
                    def hi_at(j):
                        hi(j, base + UP_SLABS * it + j - RING + 1, base // RING + UP_SLABS // RING * it + j // RING + 1,
                           first=f == 0 and peeled and j < RING)

                    if peeled:
                        start_phase(p, hi_at)
                    else:
                        for j in range(8):
                            hi_at(j)
                        act.wait_ge(h_psum, UP_CHUNKS * f + it)
                        hidden_hi(it - 1)
                    for j in range(8, 12):
                        hi_at(j)
                    act.wait_ge(mm_done, base + UP_SLABS * it + 8)
                    if peeled:
                        act.wait_ge(root_ready, ROOT_OF_PHASE[p])
                    else:
                        act.wait_ge(acc_free[1], freed0[f][1] + it)
                    for t in range(TT):
                        ins = nc.scalar.activation(sg[:, t, :], acc[:, 0, t, :], ACT.Silu, scale=stat[:, RSTD + t:RSTD + t + 1])
                    ins.then_inc(acc_free[0], 1)
                    for j in range(12, 16):
                        hi_at(j)

                def hidden_hi(chunk):
                    nc.scalar.activation(h_hi[:, bass.ds(KB * chunk, KB), :], blocks[:, 0:KB, :], ACT.Copy).then_inc(hhi_ready, 1)

                up(0, True)
                with act.Fori(1, UP_CHUNKS) as it:
                    up(it, False)
                act.wait_ge(h_psum, UP_CHUNKS * (f + 1))
                hidden_hi(UP_CHUNKS - 1)
                down0 = base + UP_CHUNKS * UP_SLABS
                with act.Fori(0, BLK // 2) as i:
                    first = down0 + 2 * DOWN_SLABS * i
                    for j in range(2 * DOWN_SLABS):
                        hi(j, first + j - RING + 1, down0 // RING + 2 * DOWN_SLABS // RING * i + j // RING + 1)
                        if j == DOWN_SLABS + 4:
                            act.wait_ge(mm_done, first + DOWN_SLABS)
                            down_squares(0, 2 * i)
                    act.wait_ge(mm_done, first + 2 * DOWN_SLABS)
                    down_squares(1, 2 * i + 1)

            def hi_in(name, j, kts=SK, width=CW):
                n = MIX[name][0] + j
                hi(j, n - RING + 1, n // RING + 1, kts=kts, width=width)

            def span(name, a, b):
                for j in range(a, b):
                    hi_in(name, j)

            def produced(name):
                n0, slabs, buf, _ = MIX[name]
                act.wait_ge(mm_done, n0 + slabs)
                return buf

            def to_nat(name, use):
                buf = produced(name)
                act.wait_ge(tr_psum, use)
                for t in range(TT):
                    ins = nc.scalar.activation(nat[:, t, :], acc[:, buf, t, :], ACT.Copy, scale=stat[:, RSTD + t:RSTD + t + 1])
                ins.then_inc(acc_free[buf], 1)

            def sigmoid_glu(i):
                buf = produced(f"gt{i}")
                if i:
                    act.wait_ge(glu_ready, 1)
                for t in range(TT):
                    ins = nc.scalar.activation(sg[:, t, :], acc[:, buf, t, :], ACT.Sigmoid, scale=stat[:, RSTD + t:RSTD + t + 1])
                ins.then_inc(acc_free[buf], 1)

            def evict_tr(i, dst, src):
                act.wait_ge(tr_psum, i + 1)
                nc.scalar.activation(dst, src, ACT.Copy).then_inc(tr_evicted, 1)

            def half(i):
                return blocks[:, KB * (i % 2):KB * (i % 2) + KB, :]

            def sigmoid_gate(name, t_out):
                _, _, buf, freed = MIX[name]
                act.wait_ge(acc_free[buf], freed + 1)
                nc.scalar.activation(t_out, t_out, ACT.Sigmoid).then_inc(gate_ready, 1)

            ffn(0)
            start_phase(1, lambda j: hi_in("a0", j))
            span("gt0", 0, 8)
            span("a1", 0, 2)
            evict_tr(0, dwt[:], msc[:, 0, 0:CT * TAPS].rearrange("p (c w) -> p c w", w=TAPS))
            evict_tr(1, rel_rows[:], msc[0:HEADS, 2, 0:RELS])
            span("a1", 2, 4)
            sigmoid_glu(0)
            span("a1", 4, 8)
            span("gt1", 0, 3)
            act.wait_ge(zeros_ready, 3)
            evict_tr(2, conv_in[:, 0:KB, PAD:PAD + SEQ], half(2))
            span("gt1", 3, 8)
            for j in range(4):
                hi_in("kiwi", j, 4, NSMALL)
            sigmoid_glu(1)
            span("qk0", 0, 4)
            produced("kiwi")
            for t in range(TT):
                for a in range(2):
                    nc.scalar.activation(ki_pad[:, t, a, IDIM * a:IDIM * (a + 1)], acc[:, 0, t, 0:IDIM], ACT.Copy,
                                         scale=stat[:, RSTD + t:RSTD + t + 1])
                ins = nc.scalar.activation(small[:, t, :], acc[:, 0, t, 0:NSMALL], ACT.Copy, scale=stat[:, RSTD + t:RSTD + t + 1])
            ins.then_inc(acc_free[0], 1)
            span("qk0", 4, 7)
            evict_tr(3, conv_in[:, KB:2 * KB, PAD:PAD + SEQ], half(3))
            span("qk0", 7, 8)
            span("qk1", 0, 2)
            evict_tr(4, ki_t[:], blocks[:, 0:2, :])
            span("qk1", 2, 4)
            to_nat("qk0", 4)
            dsts = [qi_t, qi_t, q_t, q_t, k_t, k_t]
            names = [f"qk{i}" for i in range(6)] + ["v0", "v1"]
            for i in range(6):
                if i < 5:
                    span(names[i + 1], 4, 8)
                    span(names[i + 2], 0, 2)
                    evict_tr(5 + i, dsts[i][:, KB * (i % 2):KB * (i % 2) + KB, :], half(5 + i))
                    span(names[i + 2], 2, 4)
                    to_nat(names[i + 1], 6 + i)
                else:
                    span("v0", 4, 8)
                    span("v1", 0, 2)
                    evict_tr(5 + i, dsts[i][:, KB:2 * KB, :], half(5 + i))
                    span("v1", 2, 4)

            def to_v(i):
                buf = produced(f"v{i}")
                for t in range(TT):
                    ins = nc.scalar.activation(v_n[:, t, i * CW:(i + 1) * CW], acc[:, buf, t, :], ACT.Copy,
                                               scale=stat[:, RSTD + t:RSTD + t + 1])
                ins.then_inc(acc_free[buf], 1)

            def relu(u):
                n = SEQ if u % 2 == 0 else P
                act.wait_ge(dots_ready, u + 1)
                if u >= 2:
                    act.wait_ge(score_added, 2 * (u - 1))
                nc.scalar.activation(relu_d[:, u % 2, 0:2 * n], msc[:, 2 + u % 2, 0:2 * n], ACT.Relu,
                                     scale=float(IDIM) ** -0.5).then_inc(relu_ready, 1)

            to_v(0)
            span("v1", 4, 8)
            span("gc0", 0, 4)
            to_v(1)
            for j in range(4, 8):
                hi_in("gc0", j)
                if j >= 6:
                    relu(j - 6)
            for j in range(8):
                hi_in("gc1", j)
                relu(2 + j)
                if j == 2:
                    act.wait_ge(ln_centred, 1)
                    nc.scalar.activation(squares[:], conv_out[:], ACT.Square).then_inc(ln_squares, 1)
                if j == 6:
                    sigmoid_gate("gc0", gconv[:, 0])
            for j in range(8):
                hi_in("gc2", j)
                if j < 6:
                    relu(10 + j)
                if j == 1:
                    act.wait_ge(ln_var, 1)
                    nc.scalar.activation(ln_rstd[:], ln_rstd[:], ACT.Sqrt).then_inc(ln_std, 1)
                if j == 4:
                    act.wait_ge(ln_scaled, 1)
                if j in (4, 5):
                    for c in range(KB * (j - 4), KB * (j - 3)):
                        ins = nc.scalar.activation(conv_out[:, c, :], conv_out[:, c, :], ACT.Silu,
                                                   scale=vec[:, LNG + c:LNG + c + 1], bias=vec[:, LNB + c:LNB + c + 1])
                if j == 5:
                    ins.then_inc(convf_ready, 1)
                if j == 7:
                    act.wait_ge(convf_ready, 1)
                    nc.scalar.activation(conv_hi[:], conv_out[:], ACT.Copy).then_inc(convhi_ready, 1)
            for j in range(8):
                hi_in("gc3", j)
                if j == 1:
                    sigmoid_gate("gc1", gconv[:, 1])
                if j == 6:
                    sigmoid_gate("gc2", gconv[:, 2])

            def attend(k):
                if 0 <= k - 2 < HEADS:
                    act.wait_ge(pt_psum, k - 1)
                    if k - 2 >= 2:
                        act.wait_ge(pv_psum, k - 3)
                    nc.scalar.activation(p_t[:, k % 2, :], msc[:, 2, 0:SPAN], ACT.Copy).then_inc(pt_ready, 1)
                if 0 <= k - 3 < HEADS:
                    act.wait_ge(pv_psum, k - 2)
                    nc.scalar.activation(attn_hi[:, k - 3, :], msc[:, 3, SEQ * ((k - 3) % 2):SEQ * ((k - 3) % 2) + SEQ],
                                         ACT.Copy).then_inc(athi_ready, 1)

            def exponentials(k):
                if k < HEADS:
                    lg, s = logit[k % 2], k % 2 * 2
                    act.wait_ge(max_ready, k + 1)
                    nc.scalar.activation(lg[:, 0:SEQ], lg[:, 0:SEQ], ACT.Exp, bias=stat[:, NMX + s:NMX + s + 1],
                                         accum_out=stat[:, RSUM + s:RSUM + s + 1])
                    nc.scalar.activation(lg[:, SEQ:SPAN], lg[:, SEQ:SPAN], ACT.Exp, bias=stat[:, NMX + s + 1:NMX + s + 2],
                                         accum_out=stat[:, RSUM + s + 1:RSUM + s + 2]).then_inc(exp_ready, 1)

            for g in range(24):
                hi_in(f"pw{g // 4}" if g < 16 else "ga0", g % 4 if g < 16 else g - 16)
                if g == 5:
                    sigmoid_gate("gc3", gconv[:, 3])
                if g % 2 == 1 and g >= 3:
                    attend((g - 3) // 2)
                if g % 2 == 0 and g >= 4:
                    exponentials((g - 4) // 2)
            for i in range(BLK):
                span(f"wo{i}", 0, 4)
                nxt = f"ga{i + 1}" if i < BLK - 1 else "out0"
                span(nxt, 0, 2)
                sigmoid_gate(f"ga{i}", sg[:])
                span(nxt, 2, 8)
                act.wait_ge(mixed_psum, i + 1)
                if i == 0:
                    act.wait_ge(pv_psum, HEADS)
                nc.scalar.activation(mix_hi[:, KB * i:KB * i + KB, :], half(i), ACT.Copy).then_inc(mixhi_ready, 1)
            for i in range(1, BLK):
                span(f"out{i}", 0, 4)
                down_squares(produced(f"out{i - 1}"), i - 1)
                span(f"out{i}", 4, 8)
            down_squares(produced("out3"), 3)
            ffn(1)

        @block.vector
        def _(dve):
            steps = [0]

            def link(ins):
                steps[0] += 1
                ins.then_inc(dve_step, 1)
                dve.wait_ge(dve_step, steps[0])

            def lo(j, ready, kts=SK, width=CW):
                dve.wait_ge(hi_ready, ready)
                n = kts * width
                nc.vector.tensor_tensor(wlo[:, j % RING, 0:n], raw[:, j % RING, 0:n], whi[:, j % RING, 0:n],
                                        ALU.subtract).then_inc(lo_ready, 1)

            roots = [0]

            def root(dst, src, scale):
                roots[0] += 1
                nc.vector.tensor_scalar(dst, src, scale, EPS, ALU.mult, ALU.add).then_inc(root_asked, 1)
                dve.wait_ge(root_ready, roots[0])

            def post_factor(after):
                link(nc.vector.reduce_sum(stat[:, TMP:TMP + 2], fsq[:], AX.X))
                root(stat[:, RPOST:RPOST + 2], stat[:, TMP:TMP + 2], 1.0 / D)
                if after != 1.0:
                    link(nc.vector.tensor_scalar(stat[:, RPOST:RPOST + 2], stat[:, RPOST:RPOST + 2], after, None, ALU.mult))

            def add_block(b):
                for t in range(TT):
                    r = res[:, t, b * CW:(b + 1) * CW]
                    ins = nc.vector.scalar_tensor_tensor(out=r, in0=fout[:, b, t, :], scalar=stat[:, RPOST + t:RPOST + t + 1],
                                                         in1=r, op0=ALU.mult, op1=ALU.add)
                ins.then_inc(res_ready, 1)

            def act_lo_block(p, b):
                dve.wait_ge(acthi_ready, BLK * p + b + 1)
                for k in range(KB):
                    kt = KB * b + k
                    ins = nc.vector.scalar_tensor_tensor(out=act_lo[:, kt, :], in0=blocks[:, KB * (b % 2) + k, :],
                                                         scalar=vec[:, PRE[p] + kt:PRE[p] + kt + 1], in1=act_hi[:, kt, :],
                                                         op0=ALU.mult, op1=ALU.subtract)
                ins.then_inc(actlo_ready, 1)

            def row_factor(p):
                dve.wait_ge(ssq_ready, TT * (p + 1))
                root(stat[:, RSTD:RSTD + 2], stat[:, TMP:TMP + 2], 1.0 / D)

            def start_phase(p, lo_at):
                add = add_block if p else lambda b: None
                add(0)
                add(1)
                act_lo_block(p, 0)
                lo_at(0)
                lo_at(1)
                add(2)
                act_lo_block(p, 1)
                lo_at(2)
                lo_at(3)
                add(3)
                lo_at(4)
                lo_at(5)
                act_lo_block(p, 2)
                lo_at(6)
                lo_at(7)
                act_lo_block(p, 3)

            def times_gain(sub, buf, o):
                for t in range(TT):
                    dve.wait_ge(squared, TT * BLK * sub + TT * o + t + 1)
                    ins = nc.vector.tensor_tensor(fout[:, bass.ds(o, 1), t, :], acc[:, buf:buf + 1, t, :],
                                                  gpost[:, bass.ds(o * CW, CW)].rearrange("p (o n) -> p o n", o=1), ALU.mult)
                ins.then_inc(acc_free[buf], 1)

            def ffn(f):
                base, p = ffn_base[f], 2 * f

                def hidden(chunk, done):
                    dve.wait_ge(mm_done, done)
                    dve.wait_ge(acc_free[0], freed0[f][0] + chunk + 1)
                    for t in range(TT):
                        ins = nc.vector.scalar_tensor_tensor(out=nat[:, t, :], in0=acc[:, 1, t, :], scalar=stat[:, RSTD + t:RSTD + t + 1],
                                                             in1=sg[:, t, :], op0=ALU.mult, op1=ALU.mult)
                    ins.then_inc(acc_free[1], 1)

                def hidden_lo(chunk):
                    dve.wait_ge(hhi_ready, UP_CHUNKS * f + chunk + 1)
                    kts = bass.ds(KB * chunk, KB)
                    nc.vector.tensor_tensor(h_lo[:, kts, :], blocks[:, 0:KB, :], h_hi[:, kts, :], ALU.subtract).then_inc(hlo_ready, 1)

                start_phase(p, lambda j: lo(j, base + j + 1))
                row_factor(p)
                for j in range(8, 16):
                    lo(j, base + j + 1)
                with dve.Fori(1, UP_CHUNKS) as it:
                    first = base + UP_SLABS * it
                    for j in range(16):
                        lo(j, first + j + 1)
                        if j == 3:
                            hidden(it - 1, first)
                        if j == 8:
                            hidden_lo(it - 1)
                hidden(UP_CHUNKS - 1, base + UP_CHUNKS * UP_SLABS)
                hidden_lo(UP_CHUNKS - 1)
                down0 = base + UP_CHUNKS * UP_SLABS
                dve.wait_ge(gpost_full, 16 if f == 0 else 48)
                with dve.Fori(0, BLK // 2) as i:
                    first = down0 + 2 * DOWN_SLABS * i
                    for j in range(2 * DOWN_SLABS):
                        lo(j, first + j + 1)
                        if j == DOWN_SLABS + 4:
                            times_gain(2 * f, 0, 2 * i)
                    times_gain(2 * f, 1, 2 * i + 1)
                post_factor(0.5)

            def lo_in(name, j, kts=SK, width=CW):
                lo(j, MIX[name][0] + j + 1, kts, width)

            taps = [0]

            def conv(n):
                for s in range(taps[0], min(taps[0] + n, CT * TAPS)):
                    c, w = s // (2 * TAPS) * 2 + s % 2, s % (2 * TAPS) // 2
                    if s % (2 * TAPS) == 0:
                        dve.wait_ge(tr_evicted, 3 if c < KB else 4)
                    src, dst = conv_in[:, c, w:w + SEQ], conv_out[:, c, :]
                    if w == 0:
                        ins = nc.vector.tensor_scalar(dst, src, dwt[:, c, 0:1], vec[:, DWB + c:DWB + c + 1], ALU.mult, ALU.add)
                    else:
                        dve.wait_ge(conv_tap, s - 1)
                        ins = nc.vector.scalar_tensor_tensor(out=dst, in0=src, scalar=dwt[:, c, w:w + 1], in1=dst,
                                                             op0=ALU.mult, op1=ALU.add)
                    ins.then_inc(conv_tap, 1)
                taps[0] = min(taps[0] + n, CT * TAPS)

            def produced(name):
                n0, slabs, buf, _ = MIX[name]
                dve.wait_ge(mm_done, n0 + slabs)
                return buf

            def glu_scale(i):
                buf = produced(f"a{i}")
                if i:
                    dve.wait_ge(tr_psum, 3)
                for t in range(TT):
                    ins = nc.vector.tensor_scalar(nat[:, t, :], acc[:, buf, t, :], stat[:, RSTD + t:RSTD + t + 1], None, ALU.mult)
                ins.then_inc(acc_free[buf], 1)

            def glu_mult(i):
                dve.wait_ge(acc_free[1], MIX[f"gt{i}"][3] + 1)
                dve.wait_ge(acc_free[0], MIX[f"a{i}"][3] + 1)
                nc.vector.tensor_tensor(nat[:], nat[:], sg[:], ALU.mult).then_inc(glu_ready, 1)

            def gate_bias(name, g, dst):
                buf = produced(name)
                dve.wait_ge(bgate_full[g % 2], 16 * (g // 2 + 1))
                for t in range(TT):
                    ins = nc.vector.scalar_tensor_tensor(out=dst[:, t, :], in0=acc[:, buf, t, :], scalar=stat[:, RSTD + t:RSTD + t + 1],
                                                         in1=bgate[:, g % 2, :], op0=ALU.mult, op1=ALU.add)
                ins.then_inc(acc_free[buf], 1)

            def add_scores(u):
                t, n, at0 = (1, SEQ, 0) if u % 2 == 0 else (0, P, SEQ)
                dve.wait_ge(relu_ready, u + 1)
                for a, dst in ((0, score), (1, work)):
                    d, h = dst[:, at0:at0 + n], u // 2 * 2 + a
                    src, w = relu_d[:, u % 2, a * n:(a + 1) * n], small[:, t, IDIM + h:IDIM + h + 1]
                    if u < 2:
                        ins = nc.vector.tensor_scalar(d, src, w, None, ALU.mult)
                    else:
                        dve.wait_ge(score_added, 2 * (u - 2) + a + 1)
                        ins = nc.vector.scalar_tensor_tensor(out=d, in0=src, scalar=w, in1=d, op0=ALU.mult, op1=ALU.add)
                    ins.then_inc(score_added, 1)

            def top8(r):
                parts = ((0, 0, SEQ), (1, SEQ, P))
                src = score if r == 0 else work
                for i, a, n in parts:
                    ins = nc.vector.max(stat[:, MAX8 + 8 * i:MAX8 + 8 * i + 8], src[:, a:a + n])
                link(ins)
                for i, a, n in parts:
                    ins = nc.vector.match_replace(work[:, a:a + n], stat[:, MAX8 + 8 * i:MAX8 + 8 * i + 8], src[:, a:a + n], TAKEN)
                link(ins)

            def attend(k):
                if 0 <= k - 1 < HEADS:
                    lg, s = logit[(k - 1) % 2], (k - 1) % 2 * 2
                    dve.wait_ge(exp_ready, k)
                    link(nc.vector.reciprocal(stat[:, RINV + s:RINV + s + 2], stat[:, RSUM + s:RSUM + s + 2]))
                    nc.vector.tensor_scalar(lg[:, 0:SEQ], lg[:, 0:SEQ], stat[:, RINV + s:RINV + s + 1], None, ALU.mult)
                    nc.vector.tensor_scalar(lg[:, SEQ:SPAN], lg[:, SEQ:SPAN], stat[:, RINV + s + 1:RINV + s + 2], None,
                                            ALU.mult).then_inc(prob_ready, 1)
                if 0 <= k - 3 < HEADS:
                    h = k - 3
                    dve.wait_ge(athi_ready, h + 1)
                    nc.vector.tensor_tensor(attn_lo[:, h, :], msc[:, 3, SEQ * (h % 2):SEQ * (h % 2) + SEQ], attn_hi[:, h, :],
                                            ALU.subtract).then_inc(atlo_ready, 1)
                if k < HEADS:
                    lg, s = logit[k % 2], k % 2 * 2
                    dve.wait_ge(logit_psum, k + 1)
                    if k >= 2:
                        dve.wait_ge(pt_psum, k - 1)
                    link(nc.vector.scalar_tensor_tensor(out=lg[:], in0=msc[:, k % 2, 0:SPAN], scalar=float(HD) ** -0.5,
                                                        in1=bias[:, k, :], op0=ALU.mult, op1=ALU.add))
                    for i, a, n in ((0, 0, SEQ), (1, SEQ, P)):
                        ins = nc.vector.tensor_tensor_reduce(out=lg[:, a:a + n], in0=lg[:, a:a + n], in1=addmask[:, a:a + n],
                                                             scale=1.0, scalar=2 * TAKEN, op0=ALU.add, op1=ALU.max,
                                                             accum_out=stat[:, MX + s + i:MX + s + i + 1])
                    link(ins)
                    nc.vector.tensor_scalar(stat[:, NMX + s:NMX + s + 2], stat[:, MX + s:MX + s + 2], -1.0, None,
                                            ALU.mult).then_inc(max_ready, 1)

            dve.wait_ge(vec_psum, 1)
            nc.vector.tensor_copy(vec[:, 0:NVEC], acc[:, 1, 0, 0:NVEC]).then_inc(vec_ready, 1)
            dve.wait_ge(vec_ready, 1)
            ffn(0)
            start_phase(1, lambda j: lo_in("a0", j))
            row_factor(1)
            for j in range(8):
                lo_in("gt0", j)
                if j == 4:
                    glu_scale(0)
            for j in range(8):
                lo_in("a1", j)
                if j == 5:
                    glu_mult(0)
            for j in range(8):
                lo_in("gt1", j)
                if j == 4:
                    glu_scale(1)
                if j > 5:
                    conv(4)
            for j in range(4):
                lo_in("kiwi", j, 4, NSMALL)
            conv(4)
            for j in range(8):
                lo_in("qk0", j)
                if j == 0:
                    glu_mult(1)
                conv(4)
            dve.wait_ge(acc_free[0], MIX["kiwi"][3] + 1)
            link(nc.vector.tensor_scalar(small[:, :, IDIM:NSMALL], small[:, :, IDIM:NSMALL], float(IH) ** -0.5, None, ALU.mult))
            for name in [f"qk{i}" for i in range(1, 6)] + ["v0", "v1"]:
                for j in range(8):
                    lo_in(name, j)
                    conv(4)
            conv(CT * TAPS)
            for j in range(8):
                lo_in("gc0", j)
                if j >= 6:
                    add_scores(j - 6)
            for j in range(8):
                lo_in("gc1", j)
                if j == 1:
                    dve.wait_ge(ln_psum, 1)
                    mu = msc[:, 0:1, 0:SEQ].to_broadcast([P, CT, SEQ])
                    nc.vector.tensor_tensor(conv_out[:], conv_out[:], mu, ALU.subtract).then_inc(ln_centred, 1)
                add_scores(2 + j)
                if j == 4:
                    gate_bias("gc0", 0, gconv[:, 0])
            for j in range(8):
                lo_in("gc2", j)
                if j == 0:
                    dve.wait_ge(ln_psum, 2)
                    nc.vector.tensor_scalar(ln_rstd[:, 0, :], msc[:, 1, 0:SEQ], EPS, None, ALU.add).then_inc(ln_var, 1)
                if j == 3:
                    dve.wait_ge(ln_std, 1)
                    link(nc.vector.reciprocal(ln_rstd[:], ln_rstd[:]))
                    nc.vector.tensor_tensor(conv_out[:], conv_out[:], ln_rstd[:].to_broadcast([P, CT, SEQ]),
                                            ALU.mult).then_inc(ln_scaled, 1)
                if j < 6:
                    add_scores(10 + j)
                if j == 5:
                    gate_bias("gc1", 1, gconv[:, 1])
                if j == 6:
                    dve.wait_ge(score_added, 2 * IH)
                    nc.vector.tensor_tensor(score[:], score[:], work[:], ALU.add).then_inc(score_added, 1)
            dve.wait_ge(score_masked, 1)
            for j in range(8):
                lo_in("gc3", j)
                top8(j)
                if j == 0:
                    dve.wait_ge(convhi_ready, 1)
                    nc.vector.tensor_tensor(conv_lo[:], conv_out[:], conv_hi[:], ALU.subtract).then_inc(convlo_ready, 1)
                if j == 4:
                    gate_bias("gc2", 2, gconv[:, 2])
            link(nc.vector.tensor_tensor(addmask[:], work[:], score[:], ALU.is_equal))
            nc.vector.tensor_scalar(addmask[:], addmask[:], MASKED, None, ALU.mult).then_inc(sel_ready, 1)
            dve.wait_ge(bias_full, 32 * HEADS)

            def gate_conv(i):
                buf = produced(f"pw{i}")
                dve.wait_ge(gate_ready, i + 1)
                nc.vector.tensor_tensor(gconv[:, i], gconv[:, i], acc[:, buf], ALU.mult).then_inc(acc_free[buf], 1)

            for g in range(24):
                lo_in(f"pw{g // 4}" if g < 16 else "ga0", g % 4 if g < 16 else g - 16)
                if g == 3:
                    gate_bias("gc3", 3, gconv[:, 3])
                    dve.wait_ge(mask_ready, 1)
                if g % 4 == 3 and 7 <= g < 20:
                    gate_conv(g // 4 - 1)
                if g % 2 == 1 and g >= 3:
                    attend((g - 3) // 2)
            for i in range(BLK):
                for j in range(4):
                    lo_in(f"wo{i}", j)
                gate_bias(f"ga{i}", BLK + i, sg)
                nxt = f"ga{i + 1}" if i < BLK - 1 else "out0"
                for j in range(8):
                    lo_in(nxt, j)
                    if j == 3:
                        buf = produced(f"wo{i}")
                        dve.wait_ge(gate_ready, BLK + i + 1)
                        nc.vector.tensor_tensor(sg[:], sg[:], acc[:, buf], ALU.mult).then_inc(acc_free[buf], 1)
                        dve.wait_ge(acc_free[buf], MIX[f"wo{i}"][3] + 1)
                        if i:
                            dve.wait_ge(mixed_psum, i)
                        nc.vector.tensor_tensor(nat[:], sg[:], gconv[:, i], ALU.add).then_inc(mixed_ready, 1)
                    if j == 7:
                        dve.wait_ge(mixhi_ready, i + 1)
                        nc.vector.tensor_tensor(mix_lo[:, KB * i:KB * i + KB, :], blocks[:, KB * (i % 2):KB * (i % 2) + KB, :],
                                                mix_hi[:, KB * i:KB * i + KB, :], ALU.subtract).then_inc(mixlo_ready, 1)
            dve.wait_ge(gpost_full, 32)
            for i in range(1, BLK):
                for j in range(8):
                    lo_in(f"out{i}", j)
                    if j == 3:
                        times_gain(1, MIX[f"out{i - 1}"][2], i - 1)
            times_gain(1, MIX["out3"][2], 3)
            post_factor(1.0)
            ffn(1)
            for b in range(BLK):
                add_block(b)

        @block.tensor
        def _(pe):
            def mm(o, a, b, **kw):
                return nc.tensor.matmul(o, a, b, **kw)

            def slab(j, ready, buf, hi_, lo_, first, last, kts=SK, width=CW):
                pe.wait_ge(lo_ready, ready)
                vh, vl = slot_view(whi, j % RING, kts, width), slot_view(wlo, j % RING, kts, width)
                for k in range(kts):
                    kt = first + k
                    for t in range(TT):
                        o, cols = acc[:, buf, t, 0:width], slice(t * P, (t + 1) * P)
                        mm(o, hi_[:, kt, cols], vh[:, k, :], start=kt == 0, stop=False)
                        mm(o, hi_[:, kt, cols], vl[:, k, :], start=False, stop=False)
                        ins = mm(o, lo_[:, kt, cols], vh[:, k, :], start=False, stop=kt == last)
                ins.then_inc(mm_done, 1)

            def transpose_block(src, block0, done):
                for k in range(KB):
                    for t in range(TT):
                        ins = nc.tensor.transpose(blocks[:, block0 + k, t * P:(t + 1) * P], src[:, t, k * P:(k + 1) * P], ident[:])
                ins.then_inc(done, 1)

            def act_block(p, b):
                if p == 0:
                    pe.wait_ge(x_full[b], 16)
                else:
                    pe.wait_ge(res_ready, BLK * (p - 1) + b + 1)
                if b >= 2:
                    pe.wait_ge(actlo_ready, BLK * p + b - 1)
                transpose_block(res[:, :, b * CW:(b + 1) * CW], KB * (b % 2), act_psum)

            def start_phase(p, slab_at):
                act_block(p, 0)
                act_block(p, 1)
                for b in range(BLK):
                    pe.wait_ge(actlo_ready, BLK * p + b + 1)
                    slab_at(2 * b)
                    slab_at(2 * b + 1)
                    if b < 2:
                        act_block(p, b + 2)

            def ffn(f):
                base, p = ffn_base[f], 2 * f

                def up(it, peeled):
                    def slab_at(j):
                        slab(j, base + UP_SLABS * it + j + 1, j // 8, act_hi, act_lo, (j % 8) * SK, KT - 1)

                    for m in range(2):
                        if not (peeled and f == 0):
                            pe.wait_ge(acc_free[m], freed0[f][m] + it)
                        if peeled and m == 0:
                            start_phase(p, slab_at)
                            continue
                        for j in range(8 * m, 8 * m + 8):
                            slab_at(j)
                            if j == 4 and not peeled:
                                hidden_transpose(it - 1)

                def hidden_transpose(chunk):
                    pe.wait_ge(acc_free[1], freed0[f][1] + chunk + 1)
                    transpose_block(nat[:], 0, h_psum)

                up(0, True)
                with pe.Fori(1, UP_CHUNKS) as it:
                    up(it, False)
                hidden_transpose(UP_CHUNKS - 1)
                pe.wait_ge(hlo_ready, UP_CHUNKS * (f + 1))
                down0 = base + UP_CHUNKS * UP_SLABS
                with pe.Fori(0, BLK // 2) as i:
                    for j in range(2 * DOWN_SLABS):
                        half, k = j // DOWN_SLABS, j % DOWN_SLABS
                        if k == 0:
                            pe.wait_ge(acc_free[half], freed0[f][half] + UP_CHUNKS + i)
                        slab(j, down0 + 2 * DOWN_SLABS * i + j + 1, half, h_hi, h_lo, k * SK, FT - 1)

            def slabs(name, a, b, hi_=act_hi, lo_=act_lo, kts=SK, width=CW):
                n0, count, buf, freed = MIX[name]
                if a == 0:
                    pe.wait_ge(acc_free[buf], freed)
                for j in range(a, b):
                    slab(j, n0 + j + 1, buf, hi_, lo_, j * kts, count * kts - 1, kts, width)

            def tr(i, emit):
                if i >= 2:
                    pe.wait_ge(tr_evicted, i - 1)
                emit(KB * (i % 2)).then_inc(tr_psum, 1)

            def tr_nat(i):
                def emit(b0):
                    for k in range(KB):
                        for t in range(TT):
                            ins = nc.tensor.transpose(blocks[:, b0 + k, t * P:(t + 1) * P], nat[:, t, k * P:(k + 1) * P], ident[:])
                    return ins
                tr(i, emit)

            def tr_dw(b0):
                for c in range(CT):
                    ins = nc.tensor.transpose(msc[:, 0, c * TAPS:(c + 1) * TAPS], dw_rows[:, c * P:(c + 1) * P], ident[0:TAPS, 0:TAPS])
                return ins

            def tr_rel(b0):
                return mm(msc[0:HEADS, 2, 0:RELS], relb[:], onehot[:, 0:RELS], start=True, stop=True)

            def tr_ki(b0):
                for a in range(2):
                    for t in range(TT):
                        ins = nc.tensor.transpose(blocks[:, a, t * P:(t + 1) * P], ki_pad[:, t, a, :], ident[:])
                return ins

            def dots(u):
                t, n = (1, SEQ) if u % 2 == 0 else (0, P)
                if u >= 2:
                    pe.wait_ge(relu_ready, u - 1)
                mm(msc[:, 2 + u % 2, 0:2 * n], qi_t[:, u // 2, t * P:(t + 1) * P], ki_t[:, :, 0:n],
                   start=True, stop=True).then_inc(dots_ready, 1)

            def channel_mean(bank, src):
                for c in range(CT):
                    ins = mm(msc[:, bank, 0:SEQ], mean_w[:], src[:, c, :], start=c == 0, stop=c == CT - 1)
                ins.then_inc(ln_psum, 1)

            def attend(k):
                if k < HEADS:
                    if k >= 2:
                        pe.wait_ge(max_ready, k - 1)
                    o = msc[:, k % 2, :]
                    mm(o[:, 0:SEQ], q_t[:, k, P:SEQ], k_t[:, k, :], start=True, stop=True)
                    mm(o[:, SEQ:SPAN], q_t[:, k, 0:P], k_t[:, k, 0:P], start=True, stop=True).then_inc(logit_psum, 1)
                if 0 <= k - 2 < HEADS:
                    h, lg = k - 2, logit[k % 2]
                    pe.wait_ge(prob_ready, h + 1)
                    if h:
                        pe.wait_ge(pt_ready, h)
                    nc.tensor.transpose(msc[:, 2, 0:P], lg[:, SEQ:SPAN], ident[:])
                    nc.tensor.transpose(msc[:, 2, P:SEQ], lg[:, 0:P], ident[:])
                    nc.tensor.transpose(msc[:, 2, SEQ:SPAN], lg[:, P:SEQ], ident[:]).then_inc(pt_psum, 1)
                if 0 <= k - 3 < HEADS:
                    h = k - 3
                    pe.wait_ge(pt_ready, h + 1)
                    if h:
                        pe.wait_ge(atlo_ready, h)
                    o = msc[:, 3, SEQ * (h % 2):SEQ * (h % 2) + SEQ]
                    mm(o, v_n[:, 0, h * HD:(h + 1) * HD], p_t[:, h % 2, 0:SEQ], start=True, stop=False)
                    mm(o[:, P:SEQ], v_n[:, 1, h * HD:(h + 1) * HD], p_t[:, h % 2, SEQ:SPAN], start=False,
                       stop=True).then_inc(pv_psum, 1)

            pe.wait_ge(consts_ready, 1)
            pe.wait_ge(vec_loaded, 16 * 6)
            nc.tensor.transpose(acc[:, 1, 0, 0:NVEC], vrows[0:NVEC, :], ident[0:NVEC, 0:NVEC]).then_inc(vec_psum, 1)
            ffn(0)
            pe.wait_ge(acc_free[0], MIX["a0"][3])
            start_phase(1, lambda j: slab(j, MIX["a0"][0] + j + 1, 0, act_hi, act_lo, j * SK, KT - 1))
            slabs("gt0", 0, 5)
            pe.wait_ge(mixrows_full, 48)
            tr(0, tr_dw)
            tr(1, tr_rel)
            slabs("gt0", 5, 8)
            slabs("a1", 0, 7)
            pe.wait_ge(glu_ready, 1)
            tr_nat(2)
            slabs("a1", 7, 8)
            slabs("gt1", 0, 8)
            slabs("kiwi", 0, 4, kts=4, width=NSMALL)
            slabs("qk0", 0, 3)
            pe.wait_ge(glu_ready, 2)
            tr_nat(3)
            slabs("qk0", 3, 6)
            pe.wait_ge(acc_free[0], MIX["kiwi"][3] + 1)
            tr(4, tr_ki)
            slabs("qk0", 6, 8)
            names = [f"qk{i}" for i in range(6)] + ["v0", "v1"]
            for i in range(6):
                slabs(names[i + 1], 0, 5)
                pe.wait_ge(acc_free[MIX[names[i]][2]], MIX[names[i]][3] + 1)
                tr_nat(5 + i)
                slabs(names[i + 1], 5, 8)
            slabs("v1", 0, 8)
            for j in range(8):
                slabs("gc0", j, j + 1)
                if j == 5:
                    pe.wait_ge(conv_tap, CT * TAPS)
                    channel_mean(0, conv_out)
                if j >= 2:
                    dots(j - 2)
            for j in range(8):
                slabs("gc1", j, j + 1)
                dots(6 + j)
                if j == 4:
                    pe.wait_ge(ln_squares, 1)
                    channel_mean(1, squares)
            slabs("gc2", 0, 1)
            dots(14)
            slabs("gc2", 1, 2)
            dots(15)
            slabs("gc2", 2, 8)
            slabs("gc3", 0, 8)
            attend(0)
            pe.wait_ge(convlo_ready, 1)
            for g in range(24):
                if g < 16:
                    slabs(f"pw{g // 4}", g % 4, g % 4 + 1, conv_hi, conv_lo)
                else:
                    slabs("ga0", g - 16, g - 15)
                if g % 2 == 1 and g < 20:
                    attend((g + 1) // 2)
            pe.wait_ge(atlo_ready, HEADS)
            for i in range(BLK):
                slabs(f"wo{i}", 0, 4, attn_hi, attn_lo)
                for j in range(8):
                    if i < BLK - 1:
                        slabs(f"ga{i + 1}", j, j + 1)
                    else:
                        if j == 6:
                            pe.wait_ge(mixlo_ready, BLK)
                        slabs("out0", j, j + 1, mix_hi, mix_lo)
                    if j == 3:
                        pe.wait_ge(mixed_ready, i + 1)
                        if i >= 2:
                            pe.wait_ge(mixlo_ready, i - 1)
                        transpose_block(nat[:], KB * (i % 2), mixed_psum)
            for i in range(1, BLK):
                slabs(f"out{i}", 0, 8, mix_hi, mix_lo)
            ffn(1)


_INS = ["x", "rel_bias", "ffn1_pre_g", "ffn1_wg", "ffn1_wu", "ffn1_wd", "ffn1_post_g", "mix_pre_g", "w_in",
        "b_gate", "w_o", "conv_dw", "conv_dw_b", "conv_ln_g", "conv_ln_b", "w_pw2", "w_out", "mix_post_g",
        "ffn2_pre_g", "ffn2_wg", "ffn2_wu", "ffn2_wd", "ffn2_post_g"]


def bucket_rows():
    n = np.maximum(2 * P - 1 - np.arange(RELS), 0)
    exact = BUCKETS // 2
    big = exact + (np.log(np.maximum(n, exact).astype(np.float32) / np.float32(exact)) / np.float32(np.log(P / exact))
                   * np.float32(BUCKETS - exact)).astype(np.int32)
    b = np.where(n < exact, n, np.minimum(big, BUCKETS - 1))
    return (np.arange(BUCKETS)[:, None] == b[None, :]).astype(np.float32)


def kernel(**inputs):
    import concourse.bacc as _bacc
    from concourse.bass_utils import run_bass_kernel_spmd as _run

    nc = _bacc.Bacc("TRN2", target_bir_lowering=False, num_devices=1)
    arrays, args = {}, []
    for name in _INS:
        a = np.ascontiguousarray(inputs[name])
        arrays[f"in_{name}_dram"] = a
        ap = nc.dram_tensor(f"in_{name}_dram", a.shape, mybir.dt.from_np(a.dtype), kind="ExternalInput").ap()
        args.append(ap if name == "rel_bias" else ap[0])
    arrays["in_bucket_rows_dram"] = bucket_rows()
    args.append(nc.dram_tensor("in_bucket_rows_dram", (BUCKETS, RELS), mybir.dt.float32, kind="ExternalInput").ap())
    args.append(nc.dram_tensor("bias_scratch", (HEADS, P, RELS), mybir.dt.float32).ap())
    o = nc.dram_tensor("out_0_dram", (1, SEQ, D), mybir.dt.float32, kind="ExternalOutput").ap()
    build(nc, *args, o[0])
    r = _run(nc, [arrays], core_ids=[0])
    return r.results[0]["out_0_dram"]
```

```python
import numpy as np
import concourse.bass as bass
from concourse import mybir
from contextlib import ExitStack

P = 128
D = 2048
SEQ = 256
TT = SEQ // P
KT = D // P
FF = 5632
FT = FF // P
CW = 512
EPS = 1e-6
HEADS, HD = 8, 128
IH, IDIM = 16, 64
CONV = 1024
CT = CONV // P
TAPS = 31
PAD = TAPS - 1
TOPK = 64
BUCKETS = 32
RING = 4
SK = 2
BLK = D // CW
KB = CW // P
NH = 2 * BLK
HW = CW // 2
MASKED = -1.0e30
TAKEN = -3.0e30
SPAN = 2 * P + P
RELS = 3 * P - 1
Q_AT, K_AT, V_AT, QI_AT = 0, 1024, 2048, 3072
KI_AT = 4096
GLU_AT = KI_AT + IDIM + IH
GATE_AT = GLU_AT + 2 * CONV
NSMALL = IDIM + IH

UP_CHUNKS = FF // CW
UP_SLABS = 2 * KT // SK
DOWN_SLABS = FT // SK
FFN_LEFT = UP_CHUNKS + BLK // 2
FFN_SLABS = UP_CHUNKS * UP_SLABS + BLK * DOWN_SLABS


def mix_chunks():
    plan = [("a0", 8, 0), ("gt0", 8, 1), ("kiwi", 4, 0), ("a1", 8, 1), ("gt1", 8, 0)]
    plan += [(f"qk{i}", 8, 1 - i % 2) for i in range(6)]
    plan += [(f"v{i}", 8, 1 - i) for i in range(2)]
    plan += [(f"gc{i}", 8, 1 - i % 2) for i in range(BLK)]
    plan += [(f"pw{i}", 4, 1 - i % 2) for i in range(BLK)]
    for i in range(BLK):
        plan += [(f"ga{i}", 8, 1), (f"wo{i}", 4, 0)]
    plan += [(f"out{i}", 8, 1 - i % 2) for i in range(BLK)]
    at, freed, table = FFN_SLABS, [FFN_LEFT, FFN_LEFT], {}
    for name, slabs, buf in plan:
        table[name] = (at, slabs, buf, freed[buf])
        at += slabs
        freed[buf] += 1
    return table, at, freed


MIX, MIX_END, MIX_FREED = mix_chunks()


def build(nc, x, rel_bias, f1_pre, f1_wg, f1_wu, f1_wd, f1_post, mix_pre, w_in, b_gate, w_o, conv_dw,
          conv_dw_b, ln_g, ln_b, w_pw2, w_out, mix_post, f2_pre, f2_wg, f2_wu, f2_wd, f2_post,
          bucket_rows, bias_scratch, out):
    f32, f32r = mybir.dt.float32, mybir.dt.float32r
    ALU, ACT, AX = mybir.AluOpType, mybir.ActivationFunctionType, mybir.AxisListType

    ctx = ExitStack()
    with ctx:
        at = [nc.sbuf_base + (-nc.sbuf_base) % 64]

        def sb(name, shape, dt=f32, over=None):
            size = 4 * int(np.prod(shape[1:]))
            size += -size % 32
            off = at[0] if over is None else over
            if over is None:
                at[0] += size
            return nc.alloc_sbuf_tensor_at(name, shape, dt, offset=off), off

        res, _ = sb("res", [P, TT, D])
        act_hi, o_act = sb("act_hi", [P, KT, SEQ], f32r)
        act_lo, _ = sb("act_lo", [P, KT, SEQ], f32r)
        fout, _ = sb("fout", [P, NH, TT, HW], over=o_act)
        raw, _ = sb("raw", [P, RING, SK * CW])
        whi, _ = sb("whi", [P, RING, SK * CW], f32r)
        wlo, _ = sb("wlo", [P, RING, SK * CW], f32r)
        h_hi, o_h = sb("h_hi", [P, FT, SEQ], f32r)
        h_lo, _ = sb("h_lo", [P, FT, SEQ], f32r)
        h_end = at[0]
        gpost, o_gpost = sb("gpost", [P, D])
        sg, o_sg = sb("sg", [P, TT, CW])
        nat, _ = sb("nat", [P, TT, CW])
        junk, _ = sb("junk", [P, D], over=o_sg)
        vrows, _ = sb("vrows", [P, P], over=o_sg)
        vfirst, _ = sb("vfirst", [KT, P], over=o_sg + 4 * P)
        bgate, _ = sb("bgate", [P, 2, CW])
        minus_half, _ = sb("minus_half", [P, 1])
        ident, _ = sb("ident", [P, P])
        mean_w, _ = sb("mean_w", [P, P])
        vec, _ = sb("vec", [P, 80])
        small, _ = sb("small", [P, TT, NSMALL])
        fsq, _ = sb("fsq", [P, TT, BLK])
        stat, _ = sb("stat", [P, 56])
        dwt, _ = sb("dwt", [P, CT, TAPS])
        assert at[0] <= nc.sbuf_usable_end, at[0]

        at[0] = o_h
        conv_in, o_cin = sb("conv_in", [P, CT, PAD + SEQ])
        conv_out, o_cout = sb("conv_out", [P, CT, SEQ])
        qi_t, o_qi = sb("qi_t", [P, IH // 2, SEQ])
        ki_t, _ = sb("ki_t", [P, 2, SEQ])
        q_t, o_q = sb("q_t", [P, HEADS, SEQ])
        k_t, _ = sb("k_t", [P, HEADS, SEQ])
        v_n, _ = sb("v_n", [P, TT, HEADS * HD])
        bias, _ = sb("bias", [P, HEADS, SPAN])
        gconv, o_gconv = sb("gconv", [P, BLK, TT, CW])
        score, o_score = sb("score", [P, SPAN])
        work, o_work = sb("work", [P, SPAN])
        addmask, _ = sb("addmask", [P, SPAN])
        p_t, o_pt = sb("p_t", [P, 2, SPAN])
        rel_rows, _ = sb("rel_rows", [HEADS, RELS])
        assert at[0] <= h_end, at[0]
        squares, _ = sb("squares", [P, CT, SEQ], over=o_cin)
        conv_hi, _ = sb("conv_hi", [P, CT, SEQ], f32r, over=o_cin)
        conv_lo, _ = sb("conv_lo", [P, CT, SEQ], f32r, over=o_cout)
        attn_hi, _ = sb("attn_hi", [P, HEADS, SEQ], f32r, over=o_qi)
        attn_lo, _ = sb("attn_lo", [P, HEADS, SEQ], f32r, over=o_gpost)
        mix_hi, _ = sb("mix_hi", [P, KT, SEQ], f32r, over=o_q)
        mix_lo, _ = sb("mix_lo", [P, KT, SEQ], f32r, over=o_q + KT * SEQ * 4)
        relu_d, _ = sb("relu_d", [P, 2, 2 * SEQ], over=o_sg)
        logit = [sb("logit0", [P, SPAN], over=o_score)[0], sb("logit1", [P, SPAN], over=o_work)[0]]
        ln_rstd, _ = sb("ln_rstd", [P, 1, SEQ], over=o_pt)
        ki_pad, _ = sb("ki_pad", [P, TT, 2, P], over=o_pt)
        small_t, _ = sb("small_t", [NSMALL, SEQ], over=o_pt + 4 * TT * 2 * P)
        dw_rows, _ = sb("dw_rows", [TAPS, CONV], over=o_gconv)
        onehot, _ = sb("onehot", [BUCKETS, RELS + 1], over=o_gconv + 4096)
        relb, _ = sb("relb", [BUCKETS, HEADS], over=o_gconv + 4096 + 4 * (RELS + 1))

        acc = ctx.enter_context(nc.psum_tensor("acc", [P, 2, TT, CW], f32))
        msc = ctx.enter_context(nc.psum_tensor("msc", [P, 4, CW], f32))
        blocks = msc[:].rearrange("p b (c t) -> p (b c) t", t=SEQ)

        def sem(name):
            return ctx.enter_context(nc.semaphore(name))

        raw_full = [sem(f"raw_full{i}") for i in range(RING)]
        hi_ready, lo_ready, mm_done = sem("hi_ready"), sem("lo_ready"), sem("mm_done")
        acc_free = [sem("acc_free0"), sem("acc_free1")]
        x_full = [sem(f"x_full{b}") for b in range(BLK)]
        first_loaded = sem("first_loaded")
        consts_ready, vec_loaded, vec_psum, vec_ready = sem("consts_ready"), sem("vec_loaded"), sem("vec_psum"), sem("vec_ready")
        res_ready, act_psum, acthi_ready, actlo_ready = sem("res_ready"), sem("act_psum"), sem("acthi_ready"), sem("actlo_ready")
        squared, tile0_done = sem("squared"), sem("tile0_done")
        ssq_ready, root_asked, root_ready = sem("ssq_ready"), sem("root_asked"), sem("root_ready")
        h_psum, hhi_ready, hlo_ready = sem("h_psum"), sem("hhi_ready"), sem("hlo_ready")
        gpost_full = sem("gpost_full")
        stored = sem("stored")
        dve_step = sem("dve_step")
        zeros_ready, mixrows_full = sem("zeros_ready"), sem("mixrows_full")
        tr_psum, tr_evicted = sem("tr_psum"), sem("tr_evicted")
        glu_ready = sem("glu_ready")
        bias_out, bias_full = sem("bias_out"), sem("bias_full")
        conv_tap = sem("conv_tap")
        ln_psum, ln_centred, ln_squares, ln_scaled, convf_ready, convhi_ready, convlo_ready = (
            sem("ln_psum"), sem("ln_centred"), sem("ln_squares"), sem("ln_scaled"), sem("convf_ready"),
            sem("convhi_ready"), sem("convlo_ready"))
        ln_var, ln_std = sem("ln_var"), sem("ln_std")
        dots_ready, relu_ready, score_added, score_masked, sel_ready, mask_ready = (
            sem("dots_ready"), sem("relu_ready"), sem("score_added"), sem("score_masked"),
            sem("sel_ready"), sem("mask_ready"))
        logit_psum, max_ready, exp_ready, prob_ready, pt_psum, pt_ready, pv_psum, athi_ready, atlo_ready = (
            sem("logit_psum"), sem("max_ready"), sem("exp_ready"), sem("prob_ready"), sem("pt_psum"),
            sem("pt_ready"), sem("pv_psum"), sem("athi_ready"), sem("atlo_ready"))
        bgate_full, gate_ready = [sem("bgate_full0"), sem("bgate_full1")], sem("gate_ready")
        mixed_ready, mixed_psum, mixhi_ready, mixlo_ready = sem("mixed_ready"), sem("mixed_psum"), sem("mixhi_ready"), sem("mixlo_ready")

        ROOT_OF_PHASE = [1, 3, 5]
        PRE = [0, KT, 2 * KT]
        DWB, LNG, LNB = 3 * KT, 3 * KT + CT, 3 * KT + 2 * CT
        NVEC = 2 * KT + 3 * CT
        RSTD, RPOST, TMP, MX, NMX, RSUM, RINV, MAX8 = 0, 2, 4, 8, 12, 16, 20, 32

        ffn_base = [0, MIX_END]
        freed0 = [[0, 0], MIX_FREED]
        LAST = [(FFN_SLABS, 1, BLK - 1), (MIX_END, MIX["out3"][2], BLK - 1), (MIX_END + FFN_SLABS, 1, BLK - 1)]
        w_up = [(f1_wg, f1_wu), (f2_wg, f2_wu)]
        w_down = [f1_wd, f2_wd]

        def rows(w):
            return w.rearrange("(k p) n -> p k n", p=P)

        def slot_view(t, slot, kts, width):
            return t[:, slot, 0:kts * width].rearrange("p (k n) -> p k n", n=width)

        block = ctx.enter_context(nc.Block())

        @block.sync
        def _(sp):
            def load(n, j, src, slabs_done, kts=SK, width=CW, wait=True):
                if wait:
                    sp.wait_ge(lo_ready, slabs_done)
                sp.dma_start(slot_view(raw, j % RING, kts, width), src).then_inc(raw_full[j % RING], 16)

            sp.dma_start(vfirst[:], f1_pre.rearrange("(k p) -> k p", p=P)).then_inc(first_loaded, 16)

            def load_x(b):
                xv = x.rearrange("(t p) n -> p t n", p=P)
                sp.dma_start(res[:, :, b * CW:(b + 1) * CW], xv[:, :, b * CW:(b + 1) * CW]).then_inc(x_full[b], 16)

            def ffn(f):
                base = ffn_base[f]

                def up(it):
                    for j in range(UP_SLABS):
                        if f == 0 and isinstance(it, int) and j in (0, 2, 4):
                            for b in {0: (0, 1), 2: (2,), 4: (3,)}[j]:
                                load_x(b)
                        w, k = rows(w_up[f][j // (UP_SLABS // 2)]), (j % (UP_SLABS // 2)) * SK
                        load(None, j, w[:, k:k + SK, bass.ts(it, CW)], base + UP_SLABS * it + j - RING + 1,
                             wait=not (f == 0 and isinstance(it, int) and j < RING))

                up(0)
                with sp.Fori(1, UP_CHUNKS) as it:
                    up(it)
                down0 = base + UP_CHUNKS * UP_SLABS
                for o in range(BLK):
                    for j in range(DOWN_SLABS):
                        n = DOWN_SLABS * o + j
                        load(None, n, rows(w_down[f])[:, j * SK:(j + 1) * SK, o * CW:(o + 1) * CW], down0 + n - RING + 1)

            def chunk(name, w, col, width=CW, kts=SK):
                n0, slabs, _, _ = MIX[name]
                for j in range(slabs):
                    load(n0 + j, j, rows(w)[:, j * kts:(j + 1) * kts, col:col + width], n0 + j - RING + 1, kts, width)

            ffn(0)
            chunk("a0", w_in, GLU_AT)
            chunk("gt0", w_in, GLU_AT + CONV)
            chunk("kiwi", w_in, KI_AT, NSMALL, 4)
            chunk("a1", w_in, GLU_AT + CW)
            chunk("gt1", w_in, GLU_AT + CONV + CW)
            for i, col in enumerate((QI_AT, QI_AT + CW, Q_AT, Q_AT + CW, K_AT, K_AT + CW)):
                chunk(f"qk{i}", w_in, col)
            for i in range(2):
                chunk(f"v{i}", w_in, V_AT + i * CW)
            for i in range(BLK):
                chunk(f"gc{i}", w_in, GATE_AT + D + i * CW)
            for i in range(BLK):
                chunk(f"pw{i}", w_pw2, i * CW)
            for i in range(BLK):
                chunk(f"ga{i}", w_in, GATE_AT + i * CW)
                chunk(f"wo{i}", w_o, i * CW)
            for i in range(BLK):
                chunk(f"out{i}", w_out, i * CW)
            ffn(1)
            ov = out.rearrange("(t p) n -> p t n", p=P)
            for h in range(NH):
                sp.wait_ge(res_ready, 2 * NH + h + 1)
                sp.dma_start(ov[:, :, h * HW:(h + 1) * HW], res[:, :, h * HW:(h + 1) * HW]).then_inc(stored, 16)
            sp.wait_ge(stored, 16 * NH)

        @block.gpsimd
        def _(pool):
            nc.gpsimd.memset(ident[:], 0.0).then_inc(zeros_ready, 1)
            nc.gpsimd.memset(mean_w[:], 1.0 / CONV)
            pool.wait_ge(zeros_ready, 1)
            nc.gpsimd.affine_select(out=ident[:], in_=ident[:], compare_op=ALU.not_equal, fill=1.0, base=0,
                                    pattern=[[-1, P]], channel_multiplier=1).then_inc(consts_ready, 1)

            def load_gpost(g):
                pool.dma_start(gpost[:], g.rearrange("(o n) -> o n", o=1).to_broadcast([P, D])).then_inc(gpost_full, 16)

            def root(n, t):
                pool.wait_ge(root_asked, n)
                nc.gpsimd.tensor_tensor(t, t, minus_half[:].to_broadcast([P, t.shape[-1]]), ALU.pow).then_inc(root_ready, 1)

            nc.gpsimd.memset(minus_half[:], -0.5).then_inc(zeros_ready, 1)
            pool.wait_ge(zeros_ready, 2)
            rstd, rpost = stat[:, RSTD:RSTD + 2], stat[:, RPOST:RPOST + 2]
            root(1, rstd)
            pool.wait_ge(mm_done, UP_SLABS)
            load_gpost(f1_post)
            root(2, rpost)
            pool.wait_ge(mm_done, FFN_SLABS)
            nc.gpsimd.memset(conv_in[:, :, 0:PAD], 0.0)
            nc.gpsimd.memset(ki_pad[:], 0.0).then_inc(zeros_ready, 1)
            pool.dma_start(dw_rows[:], conv_dw).then_inc(mixrows_full, 16)
            pool.dma_start(onehot[:, 0:RELS], bucket_rows).then_inc(mixrows_full, 16)
            pool.dma_start(relb[:], rel_bias).then_inc(mixrows_full, 16)
            root(3, rstd)
            pool.wait_ge(tr_evicted, 4)
            for h in range(0, HEADS, 2):
                pool.wait_ge(mm_done, MIX["qk0"][0] + 2 * h)
                pool.dma_start(bias_scratch[h:h + 2], rel_rows[h:h + 2, :].rearrange("h (o r) -> h o r", o=1)
                               .to_broadcast([2, P, RELS])).then_inc(bias_out, 16)
            pool.wait_ge(bias_out, 16 * HEADS // 2)
            for h in range(HEADS):
                skew = bass.AP(bias_scratch.tensor, h * P * RELS + P - 1, [[RELS - 1, P], [1, SEQ]])
                pool.dma_start(bias[:, h, 0:SEQ], skew).then_inc(bias_full, 16)
                skew = bass.AP(bias_scratch.tensor, h * P * RELS + 2 * P - 1, [[RELS - 1, P], [1, P]])
                pool.dma_start(bias[:, h, SEQ:SPAN], skew).then_inc(bias_full, 16)

            gates = [f"gc{i}" for i in range(BLK)] + [f"ga{i}" for i in range(BLK)]

            def load_bgate(g):
                col = (D if g < BLK else 0) + (g % BLK) * CW
                if g >= 2:
                    _, _, buf, freed = MIX[gates[g - 2]]
                    pool.wait_ge(acc_free[buf], freed + 1)
                pool.dma_start(bgate[:, g % 2, :], b_gate[col:col + CW].rearrange("(o n) -> o n", o=1)
                               .to_broadcast([P, CW])).then_inc(bgate_full[g % 2], 16)

            load_bgate(0)
            load_bgate(1)
            load_bgate(2)

            def causal(t, fill_value):
                nc.gpsimd.affine_select(out=t[:, 0:SEQ], in_=t[:, 0:SEQ], compare_op=ALU.is_ge, fill=fill_value,
                                        base=P, pattern=[[-1, SEQ]], channel_multiplier=1)
                return nc.gpsimd.affine_select(out=t[:, SEQ:SPAN], in_=t[:, SEQ:SPAN], compare_op=ALU.is_ge,
                                               fill=fill_value, base=0, pattern=[[-1, P]], channel_multiplier=1)

            pool.wait_ge(score_added, 4 * IH // 2 + 1)
            causal(score, MASKED).then_inc(score_masked, 1)
            load_bgate(3)
            pool.wait_ge(sel_ready, 1)
            causal(addmask, MASKED).then_inc(mask_ready, 1)
            for g in range(BLK, 2 * BLK):
                load_bgate(g)
            pool.wait_ge(mm_done, MIX["wo3"][0] + MIX["wo3"][1])
            load_gpost(mix_post)
            root(4, rpost)
            for buf in range(2):
                pool.wait_ge(acc_free[buf], MIX_FREED[buf])
            load_gpost(f2_post)
            root(5, rstd)
            root(6, rpost)
            for s in (gpost_full, 48), (bias_full, 32 * HEADS):
                pool.wait_ge(*s)

        @block.scalar
        def _(act):
            r = 0
            for v, n in (mix_pre, KT), (f2_pre, KT), (conv_dw_b, CT), (ln_g, CT), (ln_b, CT):
                act.dma_start(vrows[r:r + n, :], v.rearrange("(k p) -> k p", p=P)).then_inc(vec_loaded, 16)
                r += n

            def hi(j, done, loads, first=False, kts=SK, width=CW):
                act.wait_ge(raw_full[j % RING], 16 * loads)
                if not first:
                    act.wait_ge(mm_done, done)
                nc.scalar.activation(whi[:, j % RING, 0:kts * width], raw[:, j % RING, 0:kts * width],
                                     ACT.Copy).then_inc(hi_ready, 1)

            def act_hi_half(p, h):
                if p == 0 and h == 0:
                    act.wait_ge(vec_ready, 1)
                act.wait_ge(act_psum, NH * p + h + 1)
                for kt in (2 * h, 2 * h + 1):
                    ins = nc.scalar.activation(act_hi[:, kt, :], blocks[:, kt % NH, :], ACT.Copy,
                                               scale=vec[:, PRE[p] + kt:PRE[p] + kt + 1])
                ins.then_inc(acthi_ready, 1)

            def row_squares(p):
                if p == 0:
                    act.wait_ge(vec_psum, 2)
                    for b in range(BLK):
                        act.wait_ge(x_full[b], 16)
                else:
                    act.wait_ge(res_ready, NH * p)
                for t in range(TT):
                    if t:
                        act.wait_ge(ssq_ready, TT * p + t)
                    nc.scalar.activation(junk[:], res[:, t, :], ACT.Square,
                                         accum_out=stat[:, TMP + t:TMP + t + 1]).then_inc(ssq_ready, 1)

            def start_phase(p, hi_at):
                if p:
                    for j in range(RING - 1):
                        hi_at(j)
                    down_squares(*LAST[p - 1])
                    hi_at(RING - 1)
                act_hi_half(p, 0)
                act_hi_half(p, 1)
                if p == 0:
                    for j in range(RING):
                        hi_at(j)
                hi_at(4)
                act_hi_half(p, 2)
                hi_at(5)
                act_hi_half(p, 3)
                act_hi_half(p, 4)
                hi_at(6)
                act_hi_half(p, 5)
                hi_at(7)
                act_hi_half(p, 6)
                act_hi_half(p, 7)
                row_squares(p)

            def down_squares(done, buf, o):
                for t in range(TT):
                    if t == 0 and o == BLK - 1:
                        act.wait_ge(tile0_done, LAST.index((done, buf, o)) + 1)
                    else:
                        act.wait_ge(mm_done, done)
                    nc.scalar.activation(junk[:, (TT * buf + t) * CW:(TT * buf + t + 1) * CW], acc[:, buf, t, :], ACT.Square, accum_out=fsq[:, t, o:o + 1]).then_inc(squared, 1)

            def ffn(f):
                base, p = ffn_base[f], 2 * f

                def up(it, peeled):
                    def hi_at(j):
                        hi(j, base + UP_SLABS * it + j - RING + 1, base // RING + UP_SLABS // RING * it + j // RING + 1,
                           first=f == 0 and peeled and j < RING)

                    if peeled:
                        start_phase(p, hi_at)
                    else:
                        for j in range(9):
                            hi_at(j)
                        hidden_hi(it - 1)
                    for j in range(8 if peeled else 9, 12):
                        hi_at(j)
                    act.wait_ge(mm_done, base + UP_SLABS * it + 8)
                    if peeled:
                        act.wait_ge(root_ready, ROOT_OF_PHASE[p])
                    else:
                        act.wait_ge(acc_free[1], freed0[f][1] + it)
                    for t in range(TT):
                        ins = nc.scalar.activation(sg[:, t, :], acc[:, 0, t, :], ACT.Silu, scale=stat[:, RSTD + t:RSTD + t + 1])
                    ins.then_inc(acc_free[0], 1)
                    for j in range(12, 16):
                        hi_at(j)

                def hidden_hi(chunk):
                    act.wait_ge(h_psum, UP_CHUNKS * f + chunk + 1)
                    nc.scalar.activation(h_hi[:, bass.ds(KB * chunk, KB), :], blocks[:, 0:KB, :], ACT.Copy).then_inc(hhi_ready, 1)

                up(0, True)
                with act.Fori(1, UP_CHUNKS) as it:
                    up(it, False)
                down0 = base + UP_CHUNKS * UP_SLABS
                for o in range(BLK):
                    for j in range(DOWN_SLABS):
                        n = DOWN_SLABS * o + j
                        hi(n, down0 + n - RING + 1, (down0 + n) // RING + 1)
                        if o == 0 and j == 8:
                            hidden_hi(UP_CHUNKS - 1)
                        if o and j == 3:
                            down_squares(down0 + DOWN_SLABS * o, (o - 1) % 2, o - 1)

            def hi_in(name, j, kts=SK, width=CW):
                n = MIX[name][0] + j
                hi(j, n - RING + 1, n // RING + 1, kts=kts, width=width)

            def span(name, a, b):
                for j in range(a, b):
                    hi_in(name, j)

            def produced(name):
                n0, slabs, buf, _ = MIX[name]
                act.wait_ge(mm_done, n0 + slabs)
                return buf

            def to_nat(name, use):
                buf = produced(name)
                act.wait_ge(tr_psum, use)
                for t in range(TT):
                    ins = nc.scalar.activation(nat[:, t, :], acc[:, buf, t, :], ACT.Copy, scale=stat[:, RSTD + t:RSTD + t + 1])
                ins.then_inc(acc_free[buf], 1)

            def sigmoid_glu(i):
                buf = produced(f"gt{i}")
                if i:
                    act.wait_ge(glu_ready, 1)
                else:
                    act.wait_ge(zeros_ready, 3)
                for t in range(TT):
                    ins = nc.scalar.activation(sg[:, t, :], acc[:, buf, t, :], ACT.Sigmoid, scale=stat[:, RSTD + t:RSTD + t + 1])
                ins.then_inc(acc_free[buf], 1)

            def evict_tr(i, dst, src):
                act.wait_ge(tr_psum, i + 1)
                nc.scalar.activation(dst, src, ACT.Copy).then_inc(tr_evicted, 1)

            def half(i):
                return blocks[:, KB * (i % 2):KB * (i % 2) + KB, :]

            def sigmoid_gate(name, t_out):
                _, _, buf, freed = MIX[name]
                act.wait_ge(acc_free[buf], freed + 1)
                nc.scalar.activation(t_out, t_out, ACT.Sigmoid).then_inc(gate_ready, 1)

            def small_out(i):
                act.wait_ge(tr_psum, i + 1)
                for t in range(TT):
                    src = half(i)[:, 0, t * P:t * P + NSMALL]
                    for a in range(2):
                        nc.scalar.activation(ki_pad[:, t, a, IDIM * a:IDIM * (a + 1)], src[:, 0:IDIM], ACT.Copy,
                                             scale=stat[:, RSTD + t:RSTD + t + 1])
                    ins = nc.scalar.activation(small[:, t, :], src, ACT.Copy, scale=stat[:, RSTD + t:RSTD + t + 1])
                ins.then_inc(tr_evicted, 1)

            ffn(0)
            start_phase(1, lambda j: hi_in("a0", j))
            span("gt0", 0, 8)
            for j in range(4):
                hi_in("kiwi", j, 4, NSMALL)
            sigmoid_glu(0)
            evict_tr(0, dwt[:], msc[:, 0, 0:CT * TAPS].rearrange("p (c w) -> p c w", w=TAPS))
            evict_tr(1, rel_rows[:], msc[0:HEADS, 2, 0:RELS])
            span("a1", 0, 4)
            nc.scalar.activation(small_t[:], acc[0:NSMALL, produced("kiwi"), 0, 0:SEQ], ACT.Copy).then_inc(acc_free[0], 1)
            span("a1", 4, 7)
            act.wait_ge(zeros_ready, 3)
            evict_tr(2, conv_in[:, 0:KB, PAD:PAD + SEQ], half(2))
            span("a1", 7, 8)
            span("gt1", 0, 1)
            small_out(3)
            span("gt1", 1, 8)
            span("qk0", 0, 1)
            evict_tr(4, ki_t[:], half(4)[:, 0:2, :])
            span("qk0", 1, 4)
            sigmoid_glu(1)
            span("qk0", 4, 8)
            span("qk1", 0, 3)
            evict_tr(5, conv_in[:, KB:2 * KB, PAD:PAD + SEQ], half(5))
            span("qk1", 3, 4)
            to_nat("qk0", 6)
            dsts = [qi_t, qi_t, q_t, q_t, k_t, k_t]
            names = [f"qk{i}" for i in range(6)] + ["v0", "v1"]
            for i in range(6):
                if i < 5:
                    span(names[i + 1], 4, 8)
                    span(names[i + 2], 0, 2)
                    evict_tr(6 + i, dsts[i][:, KB * (i % 2):KB * (i % 2) + KB, :], half(6 + i))
                    span(names[i + 2], 2, 4)
                    to_nat(names[i + 1], 7 + i)
                else:
                    span("v0", 4, 8)
                    span("v1", 0, 2)
                    evict_tr(6 + i, dsts[i][:, KB:2 * KB, :], half(6 + i))
                    span("v1", 2, 4)

            def to_v(i):
                buf = produced(f"v{i}")
                for t in range(TT):
                    ins = nc.scalar.activation(v_n[:, t, i * CW:(i + 1) * CW], acc[:, buf, t, :], ACT.Copy,
                                               scale=stat[:, RSTD + t:RSTD + t + 1])
                ins.then_inc(acc_free[buf], 1)

            def relu(u):
                n = SEQ if u % 2 == 0 else P
                act.wait_ge(dots_ready, u + 1)
                if u >= 2:
                    act.wait_ge(score_added, 2 * (u - 1))
                nc.scalar.activation(relu_d[:, u % 2, 0:2 * n], msc[:, 2 + u % 2, 0:2 * n], ACT.Relu,
                                     scale=float(IDIM) ** -0.5).then_inc(relu_ready, 1)

            to_v(0)
            span("v1", 4, 8)
            span("gc0", 0, 4)
            to_v(1)
            for j in range(4, 8):
                hi_in("gc0", j)
                if j >= 6:
                    relu(j - 6)
            for j in range(8):
                hi_in("gc1", j)
                relu(2 + j)
                if j == 2:
                    act.wait_ge(ln_centred, 1)
                    nc.scalar.activation(squares[:], conv_out[:], ACT.Square).then_inc(ln_squares, 1)
                if j == 6:
                    sigmoid_gate("gc0", gconv[:, 0])
            for j in range(8):
                hi_in("gc2", j)
                if j < 6:
                    relu(10 + j)
                if j == 1:
                    act.wait_ge(ln_var, 1)
                    nc.scalar.activation(ln_rstd[:], ln_rstd[:], ACT.Sqrt).then_inc(ln_std, 1)
                if j == 4:
                    act.wait_ge(ln_scaled, 1)
                if j in (4, 5):
                    for c in range(KB * (j - 4), KB * (j - 3)):
                        ins = nc.scalar.activation(conv_out[:, c, :], conv_out[:, c, :], ACT.Silu,
                                                   scale=vec[:, LNG + c:LNG + c + 1], bias=vec[:, LNB + c:LNB + c + 1])
                if j == 5:
                    ins.then_inc(convf_ready, 1)
                if j == 7:
                    act.wait_ge(convf_ready, 1)
                    nc.scalar.activation(conv_hi[:], conv_out[:], ACT.Copy).then_inc(convhi_ready, 1)
            for j in range(8):
                hi_in("gc3", j)
                if j == 1:
                    sigmoid_gate("gc1", gconv[:, 1])
                if j == 6:
                    sigmoid_gate("gc2", gconv[:, 2])

            def attend(k):
                if 0 <= k - 2 < HEADS:
                    act.wait_ge(pt_psum, k - 1)
                    if k - 2 >= 2:
                        act.wait_ge(pv_psum, k - 3)
                    nc.scalar.activation(p_t[:, k % 2, :], msc[:, 2, 0:SPAN], ACT.Copy).then_inc(pt_ready, 1)
                if 0 <= k - 3 < HEADS:
                    act.wait_ge(pv_psum, k - 2)
                    nc.scalar.activation(attn_hi[:, k - 3, :], msc[:, 3, SEQ * ((k - 3) % 2):SEQ * ((k - 3) % 2) + SEQ],
                                         ACT.Copy).then_inc(athi_ready, 1)

            def exponentials(k):
                if k < HEADS:
                    lg, s = logit[k % 2], k % 2 * 2
                    act.wait_ge(max_ready, k + 1)
                    nc.scalar.activation(lg[:, 0:SEQ], lg[:, 0:SEQ], ACT.Exp, bias=stat[:, NMX + s:NMX + s + 1],
                                         accum_out=stat[:, RSUM + s:RSUM + s + 1])
                    nc.scalar.activation(lg[:, SEQ:SPAN], lg[:, SEQ:SPAN], ACT.Exp, bias=stat[:, NMX + s + 1:NMX + s + 2],
                                         accum_out=stat[:, RSUM + s + 1:RSUM + s + 2]).then_inc(exp_ready, 1)

            for g in range(24):
                hi_in(f"pw{g // 4}" if g < 16 else "ga0", g % 4 if g < 16 else g - 16)
                if g == 5:
                    sigmoid_gate("gc3", gconv[:, 3])
                if g % 2 == 1 and g >= 3:
                    attend((g - 3) // 2)
                if g % 2 == 0 and g >= 4:
                    exponentials((g - 4) // 2)
            for i in range(BLK):
                span(f"wo{i}", 0, 4)
                nxt = f"ga{i + 1}" if i < BLK - 1 else "out0"
                span(nxt, 0, 2)
                sigmoid_gate(f"ga{i}", sg[:])
                span(nxt, 2, 8)
                act.wait_ge(mixed_psum, i + 1)
                if i == 0:
                    act.wait_ge(pv_psum, HEADS)
                nc.scalar.activation(mix_hi[:, KB * i:KB * i + KB, :], half(i), ACT.Copy).then_inc(mixhi_ready, 1)
            for i in range(1, BLK):
                span(f"out{i}", 0, 4)
                down_squares(MIX[f"out{i}"][0], MIX[f"out{i - 1}"][2], i - 1)
                span(f"out{i}", 4, 8)
            ffn(1)
            down_squares(*LAST[2])

        @block.vector
        def _(dve):
            steps = [0]

            def link(ins):
                steps[0] += 1
                ins.then_inc(dve_step, 1)
                dve.wait_ge(dve_step, steps[0])

            def lo(j, ready, kts=SK, width=CW):
                dve.wait_ge(hi_ready, ready)
                n = kts * width
                nc.vector.tensor_tensor(wlo[:, j % RING, 0:n], raw[:, j % RING, 0:n], whi[:, j % RING, 0:n],
                                        ALU.subtract).then_inc(lo_ready, 1)

            roots = [0]

            def ask_root(dst, src, scale, eps):
                roots[0] += 1
                nc.vector.tensor_scalar(dst, src, scale, eps, ALU.mult, ALU.add).then_inc(root_asked, 1)

            def finish(sub):
                w = 1.0 if sub == 1 else 0.5
                dve.wait_ge(squared, TT * BLK * (sub + 1))
                link(nc.vector.reduce_sum(stat[:, TMP:TMP + 2], fsq[:], AX.X))
                ask_root(stat[:, RPOST:RPOST + 2], stat[:, TMP:TMP + 2], 1.0 / D / w ** 2, EPS / w ** 2)
                buf = LAST[sub][1]
                times_gain(sub, buf, BLK - 1)
                dve.wait_ge(root_ready, roots[0])
                dve.wait_ge(acc_free[buf], [FFN_LEFT, MIX_FREED[buf], MIX_FREED[buf] + FFN_LEFT][sub])

            def add_half(h):
                for t in range(TT):
                    r = res[:, t, h * HW:(h + 1) * HW]
                    ins = nc.vector.scalar_tensor_tensor(out=r, in0=fout[:, h, t, :], scalar=stat[:, RPOST + t:RPOST + t + 1],
                                                         in1=r, op0=ALU.mult, op1=ALU.add)
                ins.then_inc(res_ready, 1)

            def act_lo_half(p, h):
                dve.wait_ge(acthi_ready, NH * p + h + 1)
                for kt in (2 * h, 2 * h + 1):
                    ins = nc.vector.scalar_tensor_tensor(out=act_lo[:, kt, :], in0=blocks[:, kt % NH, :],
                                                         scalar=vec[:, PRE[p] + kt:PRE[p] + kt + 1], in1=act_hi[:, kt, :],
                                                         op0=ALU.mult, op1=ALU.subtract)
                ins.then_inc(actlo_ready, 1)

            def row_factor(p):
                dve.wait_ge(ssq_ready, TT * (p + 1))
                ask_root(stat[:, RSTD:RSTD + 2], stat[:, TMP:TMP + 2], 1.0 / D, EPS)
                dve.wait_ge(root_ready, roots[0])

            def start_phase(p, lo_at):
                add = add_half if p else lambda h: None
                split = lambda h: act_lo_half(p, h)
                if p:
                    for j in range(RING - 1):
                        lo_at(j)
                    finish(p - 1)
                add(0)
                add(1)
                split(0)
                add(2)
                split(1)
                if p == 0:
                    for j in range(RING - 1):
                        lo_at(j)
                add(3)
                lo_at(3)
                add(4)
                split(2)
                lo_at(4)
                split(3)
                add(5)
                split(4)
                lo_at(5)
                add(6)
                split(5)
                lo_at(6)
                add(7)
                if p == 0:
                    dve.wait_ge(vec_psum, 2)
                    nc.vector.tensor_copy(vec[:, KT:KT + NVEC], acc[:, 1, 0, 0:NVEC]).then_inc(vec_ready, 1)
                lo_at(7)
                split(6)
                split(7)

            def times_gain(sub, buf, o):
                for t in range(TT):
                    dve.wait_ge(squared, TT * BLK * sub + TT * o + t + 1)
                    ins = nc.vector.tensor_tensor(fout[:, 2 * o:2 * o + 2, t, :], acc[:, buf, t, :].rearrange("p (h n) -> p h n", n=HW),
                                                  gpost[:, o * CW:(o + 1) * CW].rearrange("p (h n) -> p h n", n=HW), ALU.mult)
                ins.then_inc(acc_free[buf], 1)

            def ffn(f):
                base, p = ffn_base[f], 2 * f

                def hidden(chunk, done):
                    dve.wait_ge(mm_done, done)
                    dve.wait_ge(acc_free[0], freed0[f][0] + chunk + 1)
                    for t in range(TT):
                        ins = nc.vector.scalar_tensor_tensor(out=nat[:, t, :], in0=acc[:, 1, t, :], scalar=stat[:, RSTD + t:RSTD + t + 1],
                                                             in1=sg[:, t, :], op0=ALU.mult, op1=ALU.mult)
                    ins.then_inc(acc_free[1], 1)

                def hidden_lo(chunk):
                    dve.wait_ge(hhi_ready, UP_CHUNKS * f + chunk + 1)
                    kts = bass.ds(KB * chunk, KB)
                    nc.vector.tensor_tensor(h_lo[:, kts, :], blocks[:, 0:KB, :], h_hi[:, kts, :], ALU.subtract).then_inc(hlo_ready, 1)

                start_phase(p, lambda j: lo(j, base + j + 1))
                row_factor(p)
                for j in range(8, 16):
                    lo(j, base + j + 1)
                with dve.Fori(1, UP_CHUNKS) as it:
                    first = base + UP_SLABS * it
                    for j in range(16):
                        lo(j, first + j + 1)
                        if j == 3:
                            hidden(it - 1, first)
                        if j == 9:
                            hidden_lo(it - 1)
                down0 = base + UP_CHUNKS * UP_SLABS
                dve.wait_ge(gpost_full, 16 if f == 0 else 48)
                for o in range(BLK):
                    for j in range(DOWN_SLABS):
                        n = DOWN_SLABS * o + j
                        lo(n, down0 + n + 1)
                        if o == 0 and j == 3:
                            hidden(UP_CHUNKS - 1, down0)
                        if o == 0 and j == 9:
                            hidden_lo(UP_CHUNKS - 1)
                        if o and j == 4:
                            times_gain(2 * f, (o - 1) % 2, o - 1)

            def lo_in(name, j, kts=SK, width=CW):
                lo(j, MIX[name][0] + j + 1, kts, width)

            taps = [0]

            def conv(n):
                for s in range(taps[0], min(taps[0] + n, CT * TAPS)):
                    c, w = s // (2 * TAPS) * 2 + s % 2, s % (2 * TAPS) // 2
                    if s % (2 * TAPS) == 0:
                        dve.wait_ge(tr_evicted, 3 if c < KB else 6)
                    src, dst = conv_in[:, c, w:w + SEQ], conv_out[:, c, :]
                    if w == 0:
                        ins = nc.vector.tensor_scalar(dst, src, dwt[:, c, 0:1], vec[:, DWB + c:DWB + c + 1], ALU.mult, ALU.add)
                    else:
                        dve.wait_ge(conv_tap, s - 1)
                        ins = nc.vector.scalar_tensor_tensor(out=dst, in0=src, scalar=dwt[:, c, w:w + 1], in1=dst,
                                                             op0=ALU.mult, op1=ALU.add)
                    ins.then_inc(conv_tap, 1)
                taps[0] = min(taps[0] + n, CT * TAPS)

            def produced(name):
                n0, slabs, buf, _ = MIX[name]
                dve.wait_ge(mm_done, n0 + slabs)
                return buf

            def glu_scale(i):
                buf = produced(f"a{i}")
                if i:
                    dve.wait_ge(tr_psum, 3)
                for t in range(TT):
                    ins = nc.vector.tensor_scalar(nat[:, t, :], acc[:, buf, t, :], stat[:, RSTD + t:RSTD + t + 1], None, ALU.mult)
                ins.then_inc(acc_free[buf], 1)

            def glu_mult(i):
                for name in f"gt{i}", f"a{i}":
                    _, _, buf, freed = MIX[name]
                    dve.wait_ge(acc_free[buf], freed + 1)
                nc.vector.tensor_tensor(nat[:], nat[:], sg[:], ALU.mult).then_inc(glu_ready, 1)

            def gate_bias(name, g, dst):
                buf = produced(name)
                dve.wait_ge(bgate_full[g % 2], 16 * (g // 2 + 1))
                for t in range(TT):
                    ins = nc.vector.scalar_tensor_tensor(out=dst[:, t, :], in0=acc[:, buf, t, :], scalar=stat[:, RSTD + t:RSTD + t + 1],
                                                         in1=bgate[:, g % 2, :], op0=ALU.mult, op1=ALU.add)
                ins.then_inc(acc_free[buf], 1)

            def add_scores(u):
                t, n, at0 = (1, SEQ, 0) if u % 2 == 0 else (0, P, SEQ)
                dve.wait_ge(relu_ready, u + 1)
                for a, dst in ((0, score), (1, work)):
                    d, h = dst[:, at0:at0 + n], u // 2 * 2 + a
                    src, w = relu_d[:, u % 2, a * n:(a + 1) * n], small[:, t, IDIM + h:IDIM + h + 1]
                    if u < 2:
                        ins = nc.vector.tensor_scalar(d, src, w, None, ALU.mult)
                    else:
                        dve.wait_ge(score_added, 2 * (u - 2) + a + 1)
                        ins = nc.vector.scalar_tensor_tensor(out=d, in0=src, scalar=w, in1=d, op0=ALU.mult, op1=ALU.add)
                    ins.then_inc(score_added, 1)

            def top8(r):
                parts = ((0, 0, SEQ), (1, SEQ, P))
                src = score if r == 0 else work
                for i, a, n in parts:
                    ins = nc.vector.max(stat[:, MAX8 + 8 * i:MAX8 + 8 * i + 8], src[:, a:a + n])
                link(ins)
                for i, a, n in parts:
                    ins = nc.vector.match_replace(work[:, a:a + n], stat[:, MAX8 + 8 * i:MAX8 + 8 * i + 8], src[:, a:a + n], TAKEN)
                link(ins)

            def attend(k):
                if 0 <= k - 1 < HEADS:
                    lg, s = logit[(k - 1) % 2], (k - 1) % 2 * 2
                    dve.wait_ge(exp_ready, k)
                    link(nc.vector.reciprocal(stat[:, RINV + s:RINV + s + 2], stat[:, RSUM + s:RSUM + s + 2]))
                    nc.vector.tensor_scalar(lg[:, 0:SEQ], lg[:, 0:SEQ], stat[:, RINV + s:RINV + s + 1], None, ALU.mult)
                    nc.vector.tensor_scalar(lg[:, SEQ:SPAN], lg[:, SEQ:SPAN], stat[:, RINV + s + 1:RINV + s + 2], None,
                                            ALU.mult).then_inc(prob_ready, 1)
                if 0 <= k - 3 < HEADS:
                    h = k - 3
                    dve.wait_ge(athi_ready, h + 1)
                    nc.vector.tensor_tensor(attn_lo[:, h, :], msc[:, 3, SEQ * (h % 2):SEQ * (h % 2) + SEQ], attn_hi[:, h, :],
                                            ALU.subtract).then_inc(atlo_ready, 1)
                if k < HEADS:
                    lg, s = logit[k % 2], k % 2 * 2
                    dve.wait_ge(logit_psum, k + 1)
                    if k >= 2:
                        dve.wait_ge(pt_psum, k - 1)
                    link(nc.vector.scalar_tensor_tensor(out=lg[:], in0=msc[:, k % 2, 0:SPAN], scalar=float(HD) ** -0.5,
                                                        in1=bias[:, k, :], op0=ALU.mult, op1=ALU.add))
                    for i, a, n in ((0, 0, SEQ), (1, SEQ, P)):
                        ins = nc.vector.tensor_tensor_reduce(out=lg[:, a:a + n], in0=lg[:, a:a + n], in1=addmask[:, a:a + n],
                                                             scale=1.0, scalar=2 * TAKEN, op0=ALU.add, op1=ALU.max,
                                                             accum_out=stat[:, MX + s + i:MX + s + i + 1])
                    link(ins)
                    nc.vector.tensor_scalar(stat[:, NMX + s:NMX + s + 2], stat[:, MX + s:MX + s + 2], -1.0, None,
                                            ALU.mult).then_inc(max_ready, 1)

            dve.wait_ge(vec_psum, 1)
            nc.vector.tensor_copy(vec[:, 0:KT], acc[:, 1, 0, 0:KT]).then_inc(vec_ready, 1)
            dve.wait_ge(vec_ready, 1)
            ffn(0)
            start_phase(1, lambda j: lo_in("a0", j))
            row_factor(1)
            for j in range(8):
                lo_in("gt0", j)
                if j == 4:
                    glu_scale(0)
            for j in range(4):
                lo_in("kiwi", j, 4, NSMALL)
            for j in range(8):
                lo_in("a1", j)
                if j == 1:
                    glu_mult(0)
            for j in range(8):
                lo_in("gt1", j)
                if j == 4:
                    glu_scale(1)
                if j > 5:
                    conv(4)
            for j in range(8):
                lo_in("qk0", j)
                if j == 5:
                    glu_mult(1)
                conv(4)
            dve.wait_ge(tr_evicted, 4)
            link(nc.vector.tensor_scalar(small[:, :, IDIM:NSMALL], small[:, :, IDIM:NSMALL], float(IH) ** -0.5, None, ALU.mult))
            for name in [f"qk{i}" for i in range(1, 6)] + ["v0", "v1"]:
                for j in range(8):
                    lo_in(name, j)
                    conv(4)
            conv(CT * TAPS)
            for j in range(8):
                lo_in("gc0", j)
                if j >= 6:
                    add_scores(j - 6)
            for j in range(8):
                lo_in("gc1", j)
                if j == 1:
                    dve.wait_ge(ln_psum, 1)
                    mu = msc[:, 0:1, 0:SEQ].to_broadcast([P, CT, SEQ])
                    nc.vector.tensor_tensor(conv_out[:], conv_out[:], mu, ALU.subtract).then_inc(ln_centred, 1)
                add_scores(2 + j)
                if j == 4:
                    gate_bias("gc0", 0, gconv[:, 0])
            for j in range(8):
                lo_in("gc2", j)
                if j == 0:
                    dve.wait_ge(ln_psum, 2)
                    nc.vector.tensor_scalar(ln_rstd[:, 0, :], msc[:, 1, 0:SEQ], EPS, None, ALU.add).then_inc(ln_var, 1)
                if j == 3:
                    dve.wait_ge(ln_std, 1)
                    link(nc.vector.reciprocal(ln_rstd[:], ln_rstd[:]))
                    nc.vector.tensor_tensor(conv_out[:], conv_out[:], ln_rstd[:].to_broadcast([P, CT, SEQ]),
                                            ALU.mult).then_inc(ln_scaled, 1)
                if j < 6:
                    add_scores(10 + j)
                if j == 5:
                    gate_bias("gc1", 1, gconv[:, 1])
                if j == 6:
                    dve.wait_ge(score_added, 2 * IH)
                    nc.vector.tensor_tensor(score[:], score[:], work[:], ALU.add).then_inc(score_added, 1)
            dve.wait_ge(score_masked, 1)
            for j in range(8):
                lo_in("gc3", j)
                top8(j)
                if j == 0:
                    dve.wait_ge(convhi_ready, 1)
                    nc.vector.tensor_tensor(conv_lo[:], conv_out[:], conv_hi[:], ALU.subtract).then_inc(convlo_ready, 1)
                if j == 4:
                    gate_bias("gc2", 2, gconv[:, 2])
            link(nc.vector.tensor_tensor(addmask[:], work[:], score[:], ALU.is_equal))
            nc.vector.tensor_scalar(addmask[:], addmask[:], MASKED, None, ALU.mult).then_inc(sel_ready, 1)
            dve.wait_ge(bias_full, 32 * HEADS)

            def gate_conv(i):
                buf = produced(f"pw{i}")
                dve.wait_ge(gate_ready, i + 1)
                nc.vector.tensor_tensor(gconv[:, i], gconv[:, i], acc[:, buf], ALU.mult).then_inc(acc_free[buf], 1)

            for g in range(24):
                lo_in(f"pw{g // 4}" if g < 16 else "ga0", g % 4 if g < 16 else g - 16)
                if g == 3:
                    gate_bias("gc3", 3, gconv[:, 3])
                    dve.wait_ge(mask_ready, 1)
                if g % 4 == 3 and 7 <= g < 20:
                    gate_conv(g // 4 - 1)
                if g % 2 == 1 and g >= 3:
                    attend((g - 3) // 2)
            for i in range(BLK):
                for j in range(4):
                    lo_in(f"wo{i}", j)
                gate_bias(f"ga{i}", BLK + i, sg)
                nxt = f"ga{i + 1}" if i < BLK - 1 else "out0"
                for j in range(8):
                    lo_in(nxt, j)
                    if j == 3:
                        buf = produced(f"wo{i}")
                        dve.wait_ge(gate_ready, BLK + i + 1)
                        nc.vector.tensor_tensor(sg[:], sg[:], acc[:, buf], ALU.mult).then_inc(acc_free[buf], 1)
                        dve.wait_ge(acc_free[buf], MIX[f"wo{i}"][3] + 1)
                        if i:
                            dve.wait_ge(mixed_psum, i)
                        nc.vector.tensor_tensor(nat[:], sg[:], gconv[:, i], ALU.add).then_inc(mixed_ready, 1)
                    if j == 7:
                        dve.wait_ge(mixhi_ready, i + 1)
                        nc.vector.tensor_tensor(mix_lo[:, KB * i:KB * i + KB, :], blocks[:, KB * (i % 2):KB * (i % 2) + KB, :],
                                                mix_hi[:, KB * i:KB * i + KB, :], ALU.subtract).then_inc(mixlo_ready, 1)
            dve.wait_ge(gpost_full, 32)
            for i in range(1, BLK):
                for j in range(8):
                    lo_in(f"out{i}", j)
                    if j == 3:
                        times_gain(1, MIX[f"out{i - 1}"][2], i - 1)
            ffn(1)
            finish(2)
            for h in range(NH):
                add_half(h)

        @block.tensor
        def _(pe):
            def mm(o, a, b, **kw):
                return nc.tensor.matmul(o, a, b, **kw)

            def slab(j, ready, buf, hi_, lo_, first, last, kts=SK, width=CW, final=False):
                pe.wait_ge(lo_ready, ready)
                vh, vl = slot_view(whi, j % RING, kts, width), slot_view(wlo, j % RING, kts, width)
                for t in range(TT):
                    for k in range(kts):
                        kt = first + k
                        o, cols = acc[:, buf, t, 0:width], slice(t * P, (t + 1) * P)
                        mm(o, hi_[:, kt, cols], vh[:, k, :], start=kt == 0, stop=False)
                        mm(o, hi_[:, kt, cols], vl[:, k, :], start=False, stop=False)
                        ins = mm(o, lo_[:, kt, cols], vh[:, k, :], start=False, stop=kt == last)
                    if final and t == 0:
                        ins.then_inc(tile0_done, 1)
                ins.then_inc(mm_done, 1)

            def transposed(src, block0, tiles):
                for k in range(tiles):
                    for t in range(TT):
                        ins = nc.tensor.transpose(blocks[:, block0 + k, t * P:(t + 1) * P], src[:, t, k * P:(k + 1) * P], ident[:])
                return ins

            def act_half(p, h):
                if p == 0:
                    pe.wait_ge(x_full[h // 2], 16)
                else:
                    pe.wait_ge(res_ready, NH * (p - 1) + h + 1)
                if h >= BLK:
                    pe.wait_ge(actlo_ready, NH * p + h - BLK + 1)
                transposed(res[:, :, h * HW:(h + 1) * HW], 2 * h % NH, 2).then_inc(act_psum, 1)

            def start_phase(p, slab_at):
                act_half(p, 0)
                act_half(p, 1)
                for j in range(NH):
                    pe.wait_ge(actlo_ready, NH * p + j + 1)
                    slab_at(j)
                    if j < 4:
                        act_half(p, j + 2 if j < 2 else j + 3)
                    if j == 1:
                        act_half(p, 4)
                    if j == 4:
                        act_half(p, 7)
                        if p == 0:
                            pe.wait_ge(vec_loaded, 16 * 5)
                            nc.tensor.transpose(acc[:, 1, 0, 0:NVEC], vrows[0:NVEC, :], ident[0:NVEC, 0:NVEC]).then_inc(vec_psum, 1)

            def ffn(f):
                base, p = ffn_base[f], 2 * f

                def up(it, peeled):
                    def slab_at(j):
                        slab(j, base + UP_SLABS * it + j + 1, j // 8, act_hi, act_lo, (j % 8) * SK, KT - 1)

                    for m in range(2):
                        if peeled and f == 0 and m == 1:
                            pe.wait_ge(vec_ready, 2)
                        if not (peeled and f == 0):
                            pe.wait_ge(acc_free[m], freed0[f][m] + it)
                        if peeled and m == 0:
                            start_phase(p, slab_at)
                            continue
                        for j in range(8 * m, 8 * m + 8):
                            slab_at(j)
                            if j == 4 and not peeled:
                                hidden_transpose(it - 1)

                def hidden_transpose(chunk):
                    pe.wait_ge(acc_free[1], freed0[f][1] + chunk + 1)
                    transposed(nat[:], 0, KB).then_inc(h_psum, 1)

                up(0, True)
                with pe.Fori(1, UP_CHUNKS) as it:
                    up(it, False)
                down0 = base + UP_CHUNKS * UP_SLABS
                for o in range(BLK):
                    pe.wait_ge(acc_free[o % 2], freed0[f][o % 2] + UP_CHUNKS + o // 2)
                    for j in range(DOWN_SLABS):
                        n = DOWN_SLABS * o + j
                        if o == 0 and j == DOWN_SLABS - KB // SK:
                            pe.wait_ge(hlo_ready, UP_CHUNKS * (f + 1))
                        slab(n, down0 + n + 1, o % 2, h_hi, h_lo, j * SK, FT - 1,
                             final=o == BLK - 1 and j == DOWN_SLABS - 1)
                        if o == 0 and j == 4:
                            hidden_transpose(UP_CHUNKS - 1)

            def slabs(name, a, b, hi_=act_hi, lo_=act_lo, kts=SK, width=CW):
                n0, count, buf, freed = MIX[name]
                if a == 0:
                    pe.wait_ge(acc_free[buf], freed)
                for j in range(a, b):
                    slab(j, n0 + j + 1, buf, hi_, lo_, j * kts, count * kts - 1, kts, width,
                         final=name == f"out{BLK - 1}" and j == count - 1)

            def tr(i, emit):
                if i >= 2:
                    pe.wait_ge(tr_evicted, i - 1)
                emit(KB * (i % 2)).then_inc(tr_psum, 1)

            def tr_nat(i):
                tr(i, lambda b0: transposed(nat[:], b0, KB))

            def tr_dw(b0):
                for c in range(CT):
                    ins = nc.tensor.transpose(msc[:, 0, c * TAPS:(c + 1) * TAPS], dw_rows[:, c * P:(c + 1) * P], ident[0:TAPS, 0:TAPS])
                return ins

            def tr_rel(b0):
                return mm(msc[0:HEADS, 2, 0:RELS], relb[:], onehot[:, 0:RELS], start=True, stop=True)

            def tr_small(b0):
                for t in range(TT):
                    ins = nc.tensor.transpose(blocks[:, b0, t * P:t * P + NSMALL], small_t[:, t * P:(t + 1) * P],
                                              ident[0:NSMALL, 0:NSMALL])
                return ins

            def tr_ki(b0):
                pe.wait_ge(tr_evicted, 4)
                for a in range(2):
                    for t in range(TT):
                        ins = nc.tensor.transpose(blocks[:, b0 + a, t * P:(t + 1) * P], ki_pad[:, t, a, :], ident[:])
                return ins

            def dots(u):
                t, n = (1, SEQ) if u % 2 == 0 else (0, P)
                if u >= 2:
                    pe.wait_ge(relu_ready, u - 1)
                mm(msc[:, 2 + u % 2, 0:2 * n], qi_t[:, u // 2, t * P:(t + 1) * P], ki_t[:, :, 0:n],
                   start=True, stop=True).then_inc(dots_ready, 1)

            def channel_mean(bank, src):
                for c in range(CT):
                    ins = mm(msc[:, bank, 0:SEQ], mean_w[:], src[:, c, :], start=c == 0, stop=c == CT - 1)
                ins.then_inc(ln_psum, 1)

            def attend(k):
                if k < HEADS:
                    if k >= 2:
                        pe.wait_ge(max_ready, k - 1)
                    o = msc[:, k % 2, :]
                    mm(o[:, 0:SEQ], q_t[:, k, P:SEQ], k_t[:, k, :], start=True, stop=True)
                    mm(o[:, SEQ:SPAN], q_t[:, k, 0:P], k_t[:, k, 0:P], start=True, stop=True).then_inc(logit_psum, 1)
                if 0 <= k - 2 < HEADS:
                    h, lg = k - 2, logit[k % 2]
                    pe.wait_ge(prob_ready, h + 1)
                    if h:
                        pe.wait_ge(pt_ready, h)
                    nc.tensor.transpose(msc[:, 2, 0:P], lg[:, SEQ:SPAN], ident[:])
                    nc.tensor.transpose(msc[:, 2, P:SEQ], lg[:, 0:P], ident[:])
                    nc.tensor.transpose(msc[:, 2, SEQ:SPAN], lg[:, P:SEQ], ident[:]).then_inc(pt_psum, 1)
                if 0 <= k - 3 < HEADS:
                    h = k - 3
                    pe.wait_ge(pt_ready, h + 1)
                    if h:
                        pe.wait_ge(atlo_ready, h)
                    o = msc[:, 3, SEQ * (h % 2):SEQ * (h % 2) + SEQ]
                    mm(o, v_n[:, 0, h * HD:(h + 1) * HD], p_t[:, h % 2, 0:SEQ], start=True, stop=False)
                    mm(o[:, P:SEQ], v_n[:, 1, h * HD:(h + 1) * HD], p_t[:, h % 2, SEQ:SPAN], start=False,
                       stop=True).then_inc(pv_psum, 1)

            pe.wait_ge(consts_ready, 1)
            pe.wait_ge(first_loaded, 16)
            nc.tensor.transpose(acc[:, 1, 0, 0:KT], vfirst[:], ident[0:KT, 0:KT]).then_inc(vec_psum, 1)
            ffn(0)
            pe.wait_ge(acc_free[0], MIX["a0"][3])
            start_phase(1, lambda j: slab(j, MIX["a0"][0] + j + 1, 0, act_hi, act_lo, j * SK, KT - 1))
            slabs("gt0", 0, 5)
            pe.wait_ge(mixrows_full, 48)
            tr(0, tr_dw)
            tr(1, tr_rel)
            slabs("gt0", 5, 8)
            n0, _, buf, freed = MIX["kiwi"]
            pe.wait_ge(acc_free[buf], freed)
            for j in range(4):
                pe.wait_ge(lo_ready, n0 + j + 1)
                vh, vl = slot_view(whi, j, 4, NSMALL), slot_view(wlo, j, 4, NSMALL)
                for k in range(4):
                    kt, o = 4 * j + k, acc[0:NSMALL, buf, 0, 0:SEQ]
                    mm(o, vh[:, k, :], act_hi[:, kt, :], start=kt == 0, stop=False)
                    mm(o, vh[:, k, :], act_lo[:, kt, :], start=False, stop=False)
                    ins = mm(o, vl[:, k, :], act_hi[:, kt, :], start=False, stop=kt == KT - 1)
                ins.then_inc(mm_done, 1)
            slabs("a1", 0, 3)
            pe.wait_ge(glu_ready, 1)
            tr_nat(2)
            slabs("a1", 3, 5)
            pe.wait_ge(acc_free[0], MIX["kiwi"][3] + 1)
            tr(3, tr_small)
            slabs("a1", 5, 8)
            slabs("gt1", 0, 5)
            tr(4, tr_ki)
            slabs("gt1", 5, 8)
            slabs("qk0", 0, 7)
            pe.wait_ge(glu_ready, 2)
            tr_nat(5)
            slabs("qk0", 7, 8)
            names = [f"qk{i}" for i in range(6)] + ["v0", "v1"]
            for i in range(6):
                slabs(names[i + 1], 0, 5)
                pe.wait_ge(acc_free[MIX[names[i]][2]], MIX[names[i]][3] + 1)
                tr_nat(6 + i)
                slabs(names[i + 1], 5, 8)
            slabs("v1", 0, 8)
            for j in range(8):
                slabs("gc0", j, j + 1)
                if j == 5:
                    pe.wait_ge(conv_tap, CT * TAPS)
                    channel_mean(0, conv_out)
                if j >= 2:
                    dots(j - 2)
            for j in range(8):
                slabs("gc1", j, j + 1)
                dots(6 + j)
                if j == 4:
                    pe.wait_ge(ln_squares, 1)
                    channel_mean(1, squares)
            slabs("gc2", 0, 1)
            dots(14)
            slabs("gc2", 1, 2)
            dots(15)
            slabs("gc2", 2, 8)
            slabs("gc3", 0, 8)
            attend(0)
            pe.wait_ge(convlo_ready, 1)
            for g in range(24):
                if g < 16:
                    slabs(f"pw{g // 4}", g % 4, g % 4 + 1, conv_hi, conv_lo)
                else:
                    slabs("ga0", g - 16, g - 15)
                if g % 2 == 1 and g < 20:
                    attend((g + 1) // 2)
            pe.wait_ge(atlo_ready, HEADS)
            for i in range(BLK):
                slabs(f"wo{i}", 0, 4, attn_hi, attn_lo)
                for j in range(8):
                    if i < BLK - 1:
                        slabs(f"ga{i + 1}", j, j + 1)
                    else:
                        if j == 6:
                            pe.wait_ge(mixlo_ready, BLK)
                        slabs("out0", j, j + 1, mix_hi, mix_lo)
                    if j == 3:
                        pe.wait_ge(mixed_ready, i + 1)
                        if i >= 2:
                            pe.wait_ge(mixlo_ready, i - 1)
                        transposed(nat[:], KB * (i % 2), KB).then_inc(mixed_psum, 1)
            for i in range(1, BLK):
                slabs(f"out{i}", 0, 8, mix_hi, mix_lo)
            ffn(1)


_INS = ["x", "rel_bias", "ffn1_pre_g", "ffn1_wg", "ffn1_wu", "ffn1_wd", "ffn1_post_g", "mix_pre_g", "w_in",
        "b_gate", "w_o", "conv_dw", "conv_dw_b", "conv_ln_g", "conv_ln_b", "w_pw2", "w_out", "mix_post_g",
        "ffn2_pre_g", "ffn2_wg", "ffn2_wu", "ffn2_wd", "ffn2_post_g"]


def bucket_rows():
    n = np.maximum(2 * P - 1 - np.arange(RELS), 0)
    exact = BUCKETS // 2
    big = exact + (np.log(np.maximum(n, exact).astype(np.float32) / np.float32(exact)) / np.float32(np.log(P / exact))
                   * np.float32(BUCKETS - exact)).astype(np.int32)
    b = np.where(n < exact, n, np.minimum(big, BUCKETS - 1))
    return (np.arange(BUCKETS)[:, None] == b[None, :]).astype(np.float32)


def kernel(**inputs):
    import concourse.bacc as _bacc
    from concourse.bass_utils import run_bass_kernel_spmd as _run

    nc = _bacc.Bacc("TRN2", target_bir_lowering=False, num_devices=1)
    arrays, args = {}, []
    for name in _INS:
        a = np.ascontiguousarray(inputs[name])
        arrays[f"in_{name}_dram"] = a
        ap = nc.dram_tensor(f"in_{name}_dram", a.shape, mybir.dt.from_np(a.dtype), kind="ExternalInput").ap()
        args.append(ap if name == "rel_bias" else ap[0])
    arrays["in_bucket_rows_dram"] = bucket_rows()
    args.append(nc.dram_tensor("in_bucket_rows_dram", (BUCKETS, RELS), mybir.dt.float32, kind="ExternalInput").ap())
    args.append(nc.dram_tensor("bias_scratch", (HEADS, P, RELS), mybir.dt.float32).ap())
    o = nc.dram_tensor("out_0_dram", (1, SEQ, D), mybir.dt.float32, kind="ExternalOutput").ap()
    build(nc, *args, o[0])
    r = _run(nc, [arrays], core_ids=[0])
    return r.results[0]["out_0_dram"]
```

```python
import numpy as np
import concourse.bass as bass
from concourse import mybir
from contextlib import ExitStack

P = 128
D = 2048
SEQ = 256
TT = SEQ // P
KT = D // P
FF = 5632
FT = FF // P
CW = 512
EPS = 1e-6
HEADS, HD = 8, 128
IH, IDIM = 16, 64
CONV = 1024
CT = CONV // P
TAPS = 31
PAD = TAPS - 1
TOPK = 64
BUCKETS = 32
RING = 4
SK = 2
BLK = D // CW
KB = CW // P
NH = 2 * BLK
HW = CW // 2
TILED = 3
MASKED = -1.0e30
TAKEN = -3.0e30
SPAN = 2 * P + P
RELS = 3 * P - 1
Q_AT, K_AT, V_AT, QI_AT = 0, 1024, 2048, 3072
KI_AT = 4096
GLU_AT = KI_AT + IDIM + IH
GATE_AT = GLU_AT + 2 * CONV
NSMALL = IDIM + IH

UP_CHUNKS = FF // CW
UP_SLABS = 2 * KT // SK
DOWN_SLABS = FT // SK
FFN_LEFT = UP_CHUNKS + BLK // 2
FFN_SLABS = UP_CHUNKS * UP_SLABS + BLK * DOWN_SLABS


def mix_chunks():
    plan = [("a0", 8, 0), ("gt0", 8, 1), ("kiwi", 4, None), ("a1", 8, 0), ("gt1", 8, 1)]
    plan += [(f"qk{i}", 8, i % 2) for i in range(6)]
    plan += [(f"v{i}", 8, i) for i in range(2)]
    plan += [(f"gc{i}", 8, i % 2) for i in range(BLK)]
    plan += [(f"pw{i}", 4, i % 2) for i in range(BLK)]
    for i in range(BLK):
        plan += [(f"ga{i}", 8, 0), (f"wo{i}", 4, 1)]
    plan += [(f"out{i}", 8, i % 2) for i in range(BLK)]
    at, freed, table = FFN_SLABS, [FFN_LEFT, FFN_LEFT], {}
    for name, slabs, buf in plan:
        table[name] = (at, slabs, buf, None if buf is None else freed[buf])
        at += slabs
        if buf is not None:
            freed[buf] += 1
    return table, at, freed


MIX, MIX_END, MIX_FREED = mix_chunks()


def build(nc, x, rel_bias, f1_pre, f1_wg, f1_wu, f1_wd, f1_post, mix_pre, w_in, b_gate, w_o, conv_dw,
          conv_dw_b, ln_g, ln_b, w_pw2, w_out, mix_post, f2_pre, f2_wg, f2_wu, f2_wd, f2_post,
          bucket_rows, bias_scratch, out):
    f32, f32r = mybir.dt.float32, mybir.dt.float32r
    ALU, ACT, AX = mybir.AluOpType, mybir.ActivationFunctionType, mybir.AxisListType

    ctx = ExitStack()
    with ctx:
        at = [nc.sbuf_base + (-nc.sbuf_base) % 64]

        def sb(name, shape, dt=f32, over=None):
            size = 4 * int(np.prod(shape[1:]))
            size += -size % 32
            off = at[0] if over is None else over
            if over is None:
                at[0] += size
            return nc.alloc_sbuf_tensor_at(name, shape, dt, offset=off), off

        res, _ = sb("res", [P, TT, D])
        act_hi, o_act = sb("act_hi", [P, NH, TT, 2, P], f32r)
        act_lo, _ = sb("act_lo", [P, NH, TT, 2, P], f32r)
        fout, _ = sb("fout", [P, NH, TT, HW], over=o_act)
        raw, _ = sb("raw", [P, RING, SK * CW])
        whi, _ = sb("whi", [P, RING, SK * CW], f32r)
        wlo, _ = sb("wlo", [P, RING, SK * CW], f32r)
        h_hi, o_h = sb("h_hi", [P, FT, SEQ], f32r)
        h_lo, _ = sb("h_lo", [P, FT, SEQ], f32r)
        h_end = at[0]
        gpost, o_gpost = sb("gpost", [P, D])
        sg, o_sg = sb("sg", [P, TT, CW])
        nat, _ = sb("nat", [P, TT, CW])
        junk, _ = sb("junk", [P, D], over=o_sg)
        vrows, _ = sb("vrows", [P, P], over=o_sg)
        vfirst, _ = sb("vfirst", [KT, P], over=o_sg + 4 * P)
        bgate, _ = sb("bgate", [P, 2, CW])
        minus_half, _ = sb("minus_half", [P, 1])
        ident, _ = sb("ident", [P, P])
        mean_w, _ = sb("mean_w", [P, P])
        vec, _ = sb("vec", [P, 80])
        small, _ = sb("small", [P, TT, NSMALL])
        fsq, _ = sb("fsq", [P, TT, BLK])
        stat, _ = sb("stat", [P, 56])
        dwt, _ = sb("dwt", [P, CT, TAPS])
        assert at[0] <= nc.sbuf_usable_end, at[0]

        at[0] = o_h
        conv_in, o_cin = sb("conv_in", [P, CT, PAD + SEQ])
        conv_out, o_cout = sb("conv_out", [P, CT, SEQ])
        qi_t, o_qi = sb("qi_t", [P, IH // 2, SEQ])
        ki_t, _ = sb("ki_t", [P, 2, SEQ])
        q_t, o_q = sb("q_t", [P, HEADS, SEQ])
        k_t, _ = sb("k_t", [P, HEADS, SEQ])
        v_n, _ = sb("v_n", [P, TT, HEADS * HD])
        bias, _ = sb("bias", [P, HEADS, SPAN])
        gconv, o_gconv = sb("gconv", [P, BLK, TT, CW])
        score, o_score = sb("score", [P, SPAN])
        work, o_work = sb("work", [P, SPAN])
        addmask, _ = sb("addmask", [P, SPAN])
        p_t, o_pt = sb("p_t", [P, 2, SPAN])
        rel_rows, _ = sb("rel_rows", [HEADS, RELS])
        assert at[0] <= h_end, at[0]
        squares, _ = sb("squares", [P, CT, SEQ], over=o_cin)
        conv_hi, _ = sb("conv_hi", [P, CT, SEQ], f32r, over=o_cin)
        conv_lo, _ = sb("conv_lo", [P, CT, SEQ], f32r, over=o_cout)
        attn_hi, _ = sb("attn_hi", [P, HEADS, SEQ], f32r, over=o_qi)
        attn_lo, _ = sb("attn_lo", [P, HEADS, SEQ], f32r, over=o_gpost)
        mix_hi, _ = sb("mix_hi", [P, KT, SEQ], f32r, over=o_q)
        mix_lo, _ = sb("mix_lo", [P, KT, SEQ], f32r, over=o_q + KT * SEQ * 4)
        relu_d, _ = sb("relu_d", [P, 2, 2 * SEQ], over=o_sg)
        logit = [sb("logit0", [P, SPAN], over=o_score)[0], sb("logit1", [P, SPAN], over=o_work)[0]]
        ln_rstd, _ = sb("ln_rstd", [P, 1, SEQ], over=o_pt)
        ki_pad, _ = sb("ki_pad", [P, TT, 2, P], over=o_pt)
        small_t, _ = sb("small_t", [NSMALL, SEQ], over=o_pt + 4 * TT * 2 * P)
        dw_rows, _ = sb("dw_rows", [TAPS, CONV], over=o_gconv)
        onehot, _ = sb("onehot", [BUCKETS, RELS + 1], over=o_gconv + 4096)
        relb, _ = sb("relb", [BUCKETS, HEADS], over=o_gconv + 4096 + 4 * (RELS + 1))

        acc = ctx.enter_context(nc.psum_tensor("acc", [P, 2, TT, CW], f32))
        msc = ctx.enter_context(nc.psum_tensor("msc", [P, 4, CW], f32))
        blocks = msc[:].rearrange("p b (c t) -> p (b c) t", t=SEQ)

        kiwi = msc[0:NSMALL, 1, 0:SEQ]

        def block_tiles(block, a, b):
            return blocks[:, block, a * P:b * P].rearrange("p (t n) -> p t n", n=P)

        def k_tile(operand, kt, t):
            if operand is act_hi or operand is act_lo:
                return operand[:, kt // 2, t, kt % 2, :]
            return operand[:, kt, t * P:(t + 1) * P]

        def sem(name):
            return ctx.enter_context(nc.semaphore(name))

        raw_full = [sem(f"raw_full{i}") for i in range(RING)]
        hi_ready, lo_ready, mm_done = sem("hi_ready"), sem("lo_ready"), sem("mm_done")
        acc_free = [sem("acc_free0"), sem("acc_free1")]
        x_full = [sem(f"x_full{b}") for b in range(BLK)]
        first_loaded = sem("first_loaded")
        consts_ready, vec_loaded, vec_psum, vec_ready = sem("consts_ready"), sem("vec_loaded"), sem("vec_psum"), sem("vec_ready")
        res_ready, act_psum, acthi_ready, actlo_ready = sem("res_ready"), sem("act_psum"), sem("acthi_ready"), sem("actlo_ready")
        squared, tile0_done = sem("squared"), sem("tile0_done")
        ssq_ready, root_asked, root_ready = sem("ssq_ready"), sem("root_asked"), sem("root_ready")
        h_psum, hhi_ready, hlo_ready = sem("h_psum"), sem("hhi_ready"), sem("hlo_ready")
        gpost_full = sem("gpost_full")
        stored = sem("stored")
        dve_step = sem("dve_step")
        zeros_ready, mixrows_full = sem("zeros_ready"), sem("mixrows_full")
        tr_psum, tr_evicted = sem("tr_psum"), sem("tr_evicted")
        kiwi_evicted = sem("kiwi_evicted")
        glu_ready = sem("glu_ready")
        bias_out, bias_full = sem("bias_out"), sem("bias_full")
        conv_tap = sem("conv_tap")
        ln_psum, ln_centred, ln_squares, ln_scaled, convf_ready, convhi_ready, convlo_ready = (
            sem("ln_psum"), sem("ln_centred"), sem("ln_squares"), sem("ln_scaled"), sem("convf_ready"),
            sem("convhi_ready"), sem("convlo_ready"))
        ln_var, ln_std = sem("ln_var"), sem("ln_std")
        dots_ready, relu_ready, score_added, score_masked, sel_ready, mask_ready = (
            sem("dots_ready"), sem("relu_ready"), sem("score_added"), sem("score_masked"),
            sem("sel_ready"), sem("mask_ready"))
        logit_psum, max_ready, exp_ready, prob_ready, pt_psum, pt_ready, pv_psum, athi_ready, atlo_ready = (
            sem("logit_psum"), sem("max_ready"), sem("exp_ready"), sem("prob_ready"), sem("pt_psum"),
            sem("pt_ready"), sem("pv_psum"), sem("athi_ready"), sem("atlo_ready"))
        bgate_full, gate_ready = [sem("bgate_full0"), sem("bgate_full1")], sem("gate_ready")
        mixed_ready, mixed_psum, mixhi_ready, mixlo_ready = sem("mixed_ready"), sem("mixed_psum"), sem("mixhi_ready"), sem("mixlo_ready")

        ROOT_OF_PHASE = [1, 2 + TT, 3 + 2 * TT]

        def res_count(p, h, t=TT - 1):
            return (NH + TILED) * (p - 1) + (TILED * t + h + 1 if h < TILED else TILED + h + 1)

        def half_count(p, h, t=TT - 1):
            return h + 1 if p == 0 else NH + res_count(p, h, t)

        PRE = [0, KT, 2 * KT]
        DWB, LNG, LNB = 3 * KT, 3 * KT + CT, 3 * KT + 2 * CT
        NVEC = 2 * KT + 3 * CT
        RSTD, RPOST, TMP, MX, NMX, RSUM, RINV, MAX8 = 0, 2, 4, 8, 12, 16, 20, 32

        ffn_base = [0, MIX_END]
        freed0 = [[0, 0], MIX_FREED]
        LAST = [(FFN_SLABS, 1, BLK - 1), (MIX_END, MIX["out3"][2], BLK - 1), (MIX_END + FFN_SLABS, 1, BLK - 1)]
        LAST_ADDS = [(0, 2), (2, 4), (4, 6), (6, 7), (7, 8)]
        LEFT = [[FFN_LEFT, FFN_LEFT], MIX_FREED, [n + FFN_LEFT for n in MIX_FREED]]
        w_up = [(f1_wg, f1_wu), (f2_wg, f2_wu)]
        w_down = [f1_wd, f2_wd]

        def rows(w):
            return w.rearrange("(k p) n -> p k n", p=P)

        def slot_view(t, slot, kts, width):
            return t[:, slot, 0:kts * width].rearrange("p (k n) -> p k n", n=width)

        block = ctx.enter_context(nc.Block())

        @block.sync
        def _(sp):
            def load(j, src, slabs_done, kts=SK, width=CW, wait=True):
                if wait:
                    sp.wait_ge(lo_ready, slabs_done)
                sp.dma_start(slot_view(raw, j % RING, kts, width), src).then_inc(raw_full[j % RING], 16)

            FIRST_WITH = [0, 2, 3, 4]

            def load_x(b):
                xv = x.rearrange("(t p) n -> p t n", p=P)
                sp.dma_start(res[:, :, b * CW:(b + 1) * CW], xv[:, :, b * CW:(b + 1) * CW]).then_inc(x_full[b], 16)

            def ffn(f):
                base = ffn_base[f]

                def up(it):
                    for j in range(UP_SLABS):
                        if f == 0 and isinstance(it, int) and j in FIRST_WITH:
                            load_x(FIRST_WITH.index(j))
                        w, k = rows(w_up[f][j // (UP_SLABS // 2)]), (j % (UP_SLABS // 2)) * SK
                        load(j, w[:, k:k + SK, bass.ts(it, CW)], base + UP_SLABS * it + j - RING + 1,
                             wait=not (f == 0 and isinstance(it, int) and j < RING))

                up(0)
                with sp.Fori(1, UP_CHUNKS) as it:
                    up(it)
                down0 = base + UP_CHUNKS * UP_SLABS
                for o in range(BLK):
                    for j in range(DOWN_SLABS):
                        n = DOWN_SLABS * o + j
                        load(n, rows(w_down[f])[:, j * SK:(j + 1) * SK, o * CW:(o + 1) * CW], down0 + n - RING + 1)

            def chunk(name, w, col, width=CW, kts=SK):
                n0, slabs, _, _ = MIX[name]
                for j in range(slabs):
                    load(j, rows(w)[:, j * kts:(j + 1) * kts, col:col + width], n0 + j - RING + 1, kts, width)

            ffn(0)
            chunk("a0", w_in, GLU_AT)
            chunk("gt0", w_in, GLU_AT + CONV)
            chunk("kiwi", w_in, KI_AT, NSMALL, 4)
            chunk("a1", w_in, GLU_AT + CW)
            chunk("gt1", w_in, GLU_AT + CONV + CW)
            for i, col in enumerate((QI_AT, QI_AT + CW, Q_AT, Q_AT + CW, K_AT, K_AT + CW)):
                chunk(f"qk{i}", w_in, col)
            for i in range(2):
                chunk(f"v{i}", w_in, V_AT + i * CW)
            for i in range(BLK):
                chunk(f"gc{i}", w_in, GATE_AT + D + i * CW)
            for i in range(BLK):
                chunk(f"pw{i}", w_pw2, i * CW)
            for i in range(BLK):
                chunk(f"ga{i}", w_in, GATE_AT + i * CW)
                chunk(f"wo{i}", w_o, i * CW)
            for i in range(BLK):
                chunk(f"out{i}", w_out, i * CW)
            ffn(1)
            ov = out.rearrange("(t p) n -> p t n", p=P)
            stores = [(0, 0, 4), (0, 4, 8)] + [(1, *halves) for halves in LAST_ADDS]
            for t, a, b in stores:
                sp.wait_ge(res_ready, 2 * (NH + TILED) + (b if t == 0 else NH + 1 + LAST_ADDS.index((a, b))))
                sp.dma_start(ov[:, t, a * HW:b * HW], res[:, t, a * HW:b * HW]).then_inc(stored, 16)
            sp.wait_ge(stored, 16 * len(stores))

        @block.gpsimd
        def _(pool):
            nc.gpsimd.memset(ident[:], 0.0).then_inc(zeros_ready, 1)
            nc.gpsimd.memset(mean_w[:], 1.0 / CONV)
            pool.wait_ge(zeros_ready, 1)
            nc.gpsimd.affine_select(out=ident[:], in_=ident[:], compare_op=ALU.not_equal, fill=1.0, base=0,
                                    pattern=[[-1, P]], channel_multiplier=1).then_inc(consts_ready, 1)

            def load_gpost(g):
                pool.dma_start(gpost[:], g.rearrange("(o n) -> o n", o=1).to_broadcast([P, D])).then_inc(gpost_full, 16)

            def root(n, t):
                pool.wait_ge(root_asked, n)
                nc.gpsimd.tensor_tensor(t, t, minus_half[:].to_broadcast([P, t.shape[-1]]), ALU.pow).then_inc(root_ready, 1)

            nc.gpsimd.memset(minus_half[:], -0.5).then_inc(zeros_ready, 1)
            pool.wait_ge(zeros_ready, 2)
            rstd, rpost = stat[:, RSTD:RSTD + 2], [stat[:, RPOST + t:RPOST + t + 1] for t in range(TT)]
            root(1, rstd)
            pool.wait_ge(mm_done, UP_SLABS)
            load_gpost(f1_post)
            root(2, rpost[0])
            root(3, rpost[1])
            pool.wait_ge(mm_done, FFN_SLABS)
            nc.gpsimd.memset(conv_in[:, :, 0:PAD], 0.0)
            nc.gpsimd.memset(ki_pad[:], 0.0).then_inc(zeros_ready, 1)
            pool.dma_start(dw_rows[:], conv_dw).then_inc(mixrows_full, 16)
            pool.dma_start(onehot[:, 0:RELS], bucket_rows).then_inc(mixrows_full, 16)
            pool.dma_start(relb[:], rel_bias).then_inc(mixrows_full, 16)
            root(4, rstd)
            pool.wait_ge(tr_evicted, 4)
            for h in range(0, HEADS, 2):
                pool.wait_ge(mm_done, MIX["qk0"][0] + 2 * h)
                pool.dma_start(bias_scratch[h:h + 2], rel_rows[h:h + 2, :].rearrange("h (o r) -> h o r", o=1)
                               .to_broadcast([2, P, RELS])).then_inc(bias_out, 16)
            pool.wait_ge(bias_out, 16 * HEADS // 2)
            for h in range(HEADS):
                skew = bass.AP(bias_scratch.tensor, h * P * RELS + P - 1, [[RELS - 1, P], [1, SEQ]])
                pool.dma_start(bias[:, h, 0:SEQ], skew).then_inc(bias_full, 16)
                skew = bass.AP(bias_scratch.tensor, h * P * RELS + 2 * P - 1, [[RELS - 1, P], [1, P]])
                pool.dma_start(bias[:, h, SEQ:SPAN], skew).then_inc(bias_full, 16)

            gates = [f"gc{i}" for i in range(BLK)] + [f"ga{i}" for i in range(BLK)]

            def load_bgate(g):
                col = (D if g < BLK else 0) + (g % BLK) * CW
                if g >= 2:
                    _, _, buf, freed = MIX[gates[g - 2]]
                    pool.wait_ge(acc_free[buf], freed + 1)
                pool.dma_start(bgate[:, g % 2, :], b_gate[col:col + CW].rearrange("(o n) -> o n", o=1)
                               .to_broadcast([P, CW])).then_inc(bgate_full[g % 2], 16)

            load_bgate(0)
            load_bgate(1)
            load_bgate(2)

            def causal(t, fill_value):
                nc.gpsimd.affine_select(out=t[:, 0:SEQ], in_=t[:, 0:SEQ], compare_op=ALU.is_ge, fill=fill_value,
                                        base=P, pattern=[[-1, SEQ]], channel_multiplier=1)
                return nc.gpsimd.affine_select(out=t[:, SEQ:SPAN], in_=t[:, SEQ:SPAN], compare_op=ALU.is_ge,
                                               fill=fill_value, base=0, pattern=[[-1, P]], channel_multiplier=1)

            pool.wait_ge(score_added, 4 * IH // 2 + 1)
            causal(score, MASKED).then_inc(score_masked, 1)
            load_bgate(3)
            pool.wait_ge(sel_ready, 1)
            causal(addmask, MASKED).then_inc(mask_ready, 1)
            for g in range(BLK, 2 * BLK):
                load_bgate(g)
            pool.wait_ge(mm_done, MIX["wo3"][0] + MIX["wo3"][1])
            load_gpost(mix_post)
            root(5, rpost[0])
            root(6, rpost[1])
            for buf in range(2):
                pool.wait_ge(acc_free[buf], MIX_FREED[buf])
            load_gpost(f2_post)
            root(7, rstd)
            root(8, rpost[0])
            root(9, rpost[1])
            for s in (gpost_full, 48), (bias_full, 32 * HEADS):
                pool.wait_ge(*s)

        @block.scalar
        def _(act):
            act.dma_start(vfirst[:], f1_pre.rearrange("(k p) -> k p", p=P)).then_inc(first_loaded, 16)
            act.wait_ge(zeros_ready, 2)
            nc.scalar.activation(fsq[:, 0, 0:1], minus_half[:], ACT.Copy)

            def load_vectors():
                r = 0
                for v, n in (mix_pre, KT), (f2_pre, KT), (conv_dw_b, CT), (ln_g, CT), (ln_b, CT):
                    act.dma_start(vrows[r:r + n, :], v.rearrange("(k p) -> k p", p=P)).then_inc(vec_loaded, 16)
                    r += n

            def hi(j, done, loads, first=False, kts=SK, width=CW):
                act.wait_ge(raw_full[j % RING], 16 * loads)
                if not first:
                    act.wait_ge(mm_done, done)
                nc.scalar.activation(whi[:, j % RING, 0:kts * width], raw[:, j % RING, 0:kts * width],
                                     ACT.Copy).then_inc(hi_ready, 1)

            def act_hi_half(p, h, a=0, b=TT):
                if p == 0 and h == 0:
                    act.wait_ge(vec_ready, 1)
                act.wait_ge(act_psum, half_count(p, h, b - 1))
                for k in range(2):
                    kt = 2 * h + k
                    ins = nc.scalar.activation(act_hi[:, h, a:b, k, :], block_tiles(kt % NH, a, b), ACT.Copy,
                                               scale=vec[:, PRE[p] + kt:PRE[p] + kt + 1])
                ins.then_inc(acthi_ready, 1)

            def row_squares(p, t):
                if t:
                    act.wait_ge(ssq_ready, TT * p + t)
                elif p == 0:
                    act.wait_ge(vec_psum, 2)
                    for b in range(BLK):
                        act.wait_ge(x_full[b], 16)
                else:
                    act.wait_ge(res_ready, res_count(p, NH - 1))
                nc.scalar.activation(junk[:], res[:, t, :], ACT.Square,
                                     accum_out=stat[:, TMP + t:TMP + t + 1]).then_inc(ssq_ready, 1)

            def start_phase(p, hi_at):
                if p == 0:
                    for h in range(2):
                        act_hi_half(p, h)
                        hi_at(h)
                    hi_at(2)
                    load_vectors()
                    act_hi_half(p, 2)
                    hi_at(3)
                else:
                    chunk_squares(*LAST[p - 1], 0)
                    hi_at(0)
                    act_hi_half(p, 0, 0, 1)
                    act_hi_half(p, 1, 0, 1)
                    hi_at(1)
                    chunk_squares(*LAST[p - 1], 1)
                    act_hi_half(p, 2, 0, 1)
                    hi_at(2)
                    hi_at(3)
                    for h in range(TILED):
                        act_hi_half(p, h, 1, 2)
                act_hi_half(p, 3)
                hi_at(4)
                act_hi_half(p, 4)
                hi_at(5)
                act_hi_half(p, 5)
                hi_at(6)
                act_hi_half(p, 6)
                hi_at(7)
                act_hi_half(p, 7)

            def chunk_squares(done, buf, o, t):
                if t == 0 and o == BLK - 1:
                    act.wait_ge(tile0_done, LAST.index((done, buf, o)) + 1)
                else:
                    act.wait_ge(mm_done, done)
                nc.scalar.activation(junk[:, (TT * buf + t) * CW:(TT * buf + t + 1) * CW], acc[:, buf, t, :],
                                     ACT.Square, accum_out=fsq[:, t, o:o + 1]).then_inc(squared, 1)

            def down_squares(done, buf, o):
                for t in range(TT):
                    chunk_squares(done, buf, o, t)

            def ffn(f):
                base, p = ffn_base[f], 2 * f

                def up(it, peeled):
                    def hi_at(j):
                        hi(j, base + UP_SLABS * it + j - RING + 1, base // RING + UP_SLABS // RING * it + j // RING + 1,
                           first=f == 0 and peeled and j < RING)

                    if peeled:
                        start_phase(p, hi_at)
                    else:
                        for j in range(8):
                            hi_at(j)
                    for j in range(8, 12):
                        hi_at(j)
                        if j < 10 and peeled:
                            row_squares(p, j - 8)
                        if j == 8 and not peeled:
                            hidden_hi(it - 1)
                    act.wait_ge(mm_done, base + UP_SLABS * it + 8)
                    if peeled:
                        act.wait_ge(root_ready, ROOT_OF_PHASE[p])
                    else:
                        act.wait_ge(acc_free[1], freed0[f][1] + it)
                    for t in range(TT):
                        ins = nc.scalar.activation(sg[:, t, :], acc[:, 0, t, :], ACT.Silu, scale=stat[:, RSTD + t:RSTD + t + 1])
                    ins.then_inc(acc_free[0], 1)
                    for j in range(12, 16):
                        hi_at(j)

                def hidden_hi(chunk):
                    act.wait_ge(h_psum, UP_CHUNKS * f + chunk + 1)
                    nc.scalar.activation(h_hi[:, bass.ds(KB * chunk, KB), :], blocks[:, 0:KB, :], ACT.Copy).then_inc(hhi_ready, 1)

                up(0, True)
                with act.Fori(1, UP_CHUNKS) as it:
                    up(it, False)
                down0 = base + UP_CHUNKS * UP_SLABS
                for o in range(BLK):
                    for j in range(DOWN_SLABS):
                        n = DOWN_SLABS * o + j
                        hi(n, down0 + n - RING + 1, (down0 + n) // RING + 1)
                        if o == 0 and j == 8:
                            hidden_hi(UP_CHUNKS - 1)
                        if o and j == 3:
                            down_squares(down0 + DOWN_SLABS * o, (o - 1) % 2, o - 1)

            def hi_in(name, j, kts=SK, width=CW):
                n = MIX[name][0] + j
                hi(j, n - RING + 1, n // RING + 1, kts=kts, width=width)

            def span(name, a, b):
                for j in range(a, b):
                    hi_in(name, j)

            def produced(name):
                n0, slabs, buf, _ = MIX[name]
                act.wait_ge(mm_done, n0 + slabs)
                return buf

            def to_nat(name, use):
                buf = produced(name)
                act.wait_ge(tr_psum, use)
                for t in range(TT):
                    ins = nc.scalar.activation(nat[:, t, :], acc[:, buf, t, :], ACT.Copy, scale=stat[:, RSTD + t:RSTD + t + 1])
                ins.then_inc(acc_free[buf], 1)

            def sigmoid_glu(i):
                buf = produced(f"gt{i}")
                if i:
                    act.wait_ge(glu_ready, 1)
                else:
                    act.wait_ge(zeros_ready, 3)
                for t in range(TT):
                    ins = nc.scalar.activation(sg[:, t, :], acc[:, buf, t, :], ACT.Sigmoid, scale=stat[:, RSTD + t:RSTD + t + 1])
                ins.then_inc(acc_free[buf], 1)

            def evict_tr(i, dst, src):
                act.wait_ge(tr_psum, i + 1)
                nc.scalar.activation(dst, src, ACT.Copy).then_inc(tr_evicted, 1)

            def half(i):
                return blocks[:, KB * (i % 2):KB * (i % 2) + KB, :]

            def sigmoid_gate(name, t_out):
                _, _, buf, freed = MIX[name]
                act.wait_ge(acc_free[buf], freed + 1)
                nc.scalar.activation(t_out, t_out, ACT.Sigmoid).then_inc(gate_ready, 1)

            def small_out(i):
                act.wait_ge(tr_psum, i + 1)
                for t in range(TT):
                    src = half(i)[:, 0, t * P:t * P + NSMALL]
                    for a in range(2):
                        nc.scalar.activation(ki_pad[:, t, a, IDIM * a:IDIM * (a + 1)], src[:, 0:IDIM], ACT.Copy,
                                             scale=stat[:, RSTD + t:RSTD + t + 1])
                    ins = nc.scalar.activation(small[:, t, :], src, ACT.Copy, scale=stat[:, RSTD + t:RSTD + t + 1])
                ins.then_inc(tr_evicted, 1)

            ffn(0)
            start_phase(1, lambda j: hi_in("a0", j))
            for t in range(TT):
                hi_in("gt0", t)
                row_squares(1, t)
            span("gt0", TT, 8)
            for j in range(4):
                hi_in("kiwi", j, 4, NSMALL)
            sigmoid_glu(0)
            span("a1", 0, 2)
            evict_tr(0, dwt[:], msc[:, 0, 0:CT * TAPS].rearrange("p (c w) -> p c w", w=TAPS))
            evict_tr(1, rel_rows[:], msc[0:HEADS, 2, 0:RELS])
            span("a1", 2, 4)
            produced("kiwi")
            nc.scalar.activation(small_t[:], kiwi, ACT.Copy).then_inc(kiwi_evicted, 1)
            span("a1", 4, 7)
            act.wait_ge(zeros_ready, 3)
            evict_tr(2, conv_in[:, 0:KB, PAD:PAD + SEQ], half(2))
            span("a1", 7, 8)
            span("gt1", 0, 1)
            small_out(3)
            span("gt1", 1, 8)
            span("qk0", 0, 1)
            evict_tr(4, ki_t[:], half(4)[:, 0:2, :])
            span("qk0", 1, 4)
            sigmoid_glu(1)
            span("qk0", 4, 8)
            span("qk1", 0, 3)
            evict_tr(5, conv_in[:, KB:2 * KB, PAD:PAD + SEQ], half(5))
            span("qk1", 3, 4)
            to_nat("qk0", 6)
            dsts = [qi_t, qi_t, q_t, q_t, k_t, k_t]
            names = [f"qk{i}" for i in range(6)] + ["v0", "v1"]
            for i in range(6):
                if i < 5:
                    span(names[i + 1], 4, 8)
                    span(names[i + 2], 0, 2)
                    evict_tr(6 + i, dsts[i][:, KB * (i % 2):KB * (i % 2) + KB, :], half(6 + i))
                    span(names[i + 2], 2, 4)
                    to_nat(names[i + 1], 7 + i)
                else:
                    span("v0", 4, 8)
                    span("v1", 0, 2)
                    evict_tr(6 + i, dsts[i][:, KB:2 * KB, :], half(6 + i))
                    span("v1", 2, 4)

            def to_v(i):
                buf = produced(f"v{i}")
                for t in range(TT):
                    ins = nc.scalar.activation(v_n[:, t, i * CW:(i + 1) * CW], acc[:, buf, t, :], ACT.Copy,
                                               scale=stat[:, RSTD + t:RSTD + t + 1])
                ins.then_inc(acc_free[buf], 1)

            def relu(u):
                n = SEQ if u % 2 == 0 else P
                act.wait_ge(dots_ready, u + 1)
                if u >= 2:
                    act.wait_ge(score_added, 2 * (u - 1))
                nc.scalar.activation(relu_d[:, u % 2, 0:2 * n], msc[:, 2 + u % 2, 0:2 * n], ACT.Relu,
                                     scale=float(IDIM) ** -0.5).then_inc(relu_ready, 1)

            to_v(0)
            span("v1", 4, 8)
            span("gc0", 0, 4)
            to_v(1)
            for j in range(4, 8):
                hi_in("gc0", j)
                if j >= 6:
                    relu(j - 6)
            for j in range(8):
                hi_in("gc1", j)
                relu(2 + j)
                if j == 2:
                    act.wait_ge(ln_centred, 1)
                    nc.scalar.activation(squares[:], conv_out[:], ACT.Square).then_inc(ln_squares, 1)
                if j == 6:
                    sigmoid_gate("gc0", gconv[:, 0])
            for j in range(8):
                hi_in("gc2", j)
                if j < 6:
                    relu(10 + j)
                if j == 1:
                    act.wait_ge(ln_var, 1)
                    nc.scalar.activation(ln_rstd[:], ln_rstd[:], ACT.Sqrt).then_inc(ln_std, 1)
                if j == 4:
                    act.wait_ge(ln_scaled, 1)
                if j in (4, 5):
                    for c in range(KB * (j - 4), KB * (j - 3)):
                        ins = nc.scalar.activation(conv_out[:, c, :], conv_out[:, c, :], ACT.Silu,
                                                   scale=vec[:, LNG + c:LNG + c + 1], bias=vec[:, LNB + c:LNB + c + 1])
                if j == 5:
                    ins.then_inc(convf_ready, 1)
                if j == 7:
                    act.wait_ge(convf_ready, 1)
                    nc.scalar.activation(conv_hi[:], conv_out[:], ACT.Copy).then_inc(convhi_ready, 1)
            for j in range(8):
                hi_in("gc3", j)
                if j == 1:
                    sigmoid_gate("gc1", gconv[:, 1])
                if j == 6:
                    sigmoid_gate("gc2", gconv[:, 2])

            def attend(k):
                if 0 <= k - 2 < HEADS:
                    act.wait_ge(pt_psum, k - 1)
                    if k - 2 >= 2:
                        act.wait_ge(pv_psum, k - 3)
                    nc.scalar.activation(p_t[:, k % 2, :], msc[:, 2, 0:SPAN], ACT.Copy).then_inc(pt_ready, 1)
                if 0 <= k - 3 < HEADS:
                    act.wait_ge(pv_psum, k - 2)
                    nc.scalar.activation(attn_hi[:, k - 3, :], msc[:, 3, SEQ * ((k - 3) % 2):SEQ * ((k - 3) % 2) + SEQ],
                                         ACT.Copy).then_inc(athi_ready, 1)

            def exponentials(k):
                if k < HEADS:
                    lg, s = logit[k % 2], k % 2 * 2
                    act.wait_ge(max_ready, k + 1)
                    nc.scalar.activation(lg[:, 0:SEQ], lg[:, 0:SEQ], ACT.Exp, bias=stat[:, NMX + s:NMX + s + 1],
                                         accum_out=stat[:, RSUM + s:RSUM + s + 1])
                    nc.scalar.activation(lg[:, SEQ:SPAN], lg[:, SEQ:SPAN], ACT.Exp, bias=stat[:, NMX + s + 1:NMX + s + 2],
                                         accum_out=stat[:, RSUM + s + 1:RSUM + s + 2]).then_inc(exp_ready, 1)

            for g in range(24):
                hi_in(f"pw{g // 4}" if g < 16 else "ga0", g % 4 if g < 16 else g - 16)
                if g == 5:
                    sigmoid_gate("gc3", gconv[:, 3])
                if g % 2 == 1 and g >= 3:
                    attend((g - 3) // 2)
                if g % 2 == 0 and g >= 4:
                    exponentials((g - 4) // 2)
            for i in range(BLK):
                span(f"wo{i}", 0, 4)
                nxt = f"ga{i + 1}" if i < BLK - 1 else "out0"
                span(nxt, 0, 2)
                sigmoid_gate(f"ga{i}", sg[:])
                span(nxt, 2, 8)
                act.wait_ge(mixed_psum, i + 1)
                if i == 0:
                    act.wait_ge(pv_psum, HEADS)
                nc.scalar.activation(mix_hi[:, KB * i:KB * i + KB, :], half(i), ACT.Copy).then_inc(mixhi_ready, 1)
            for i in range(1, BLK):
                span(f"out{i}", 0, 4)
                down_squares(MIX[f"out{i}"][0], MIX[f"out{i - 1}"][2], i - 1)
                span(f"out{i}", 4, 8)
            ffn(1)
            down_squares(*LAST[2])

        @block.vector
        def _(dve):
            steps = [0]

            def link(ins):
                steps[0] += 1
                ins.then_inc(dve_step, 1)
                dve.wait_ge(dve_step, steps[0])

            def lo(j, ready, kts=SK, width=CW):
                dve.wait_ge(hi_ready, ready)
                n = kts * width
                nc.vector.tensor_tensor(wlo[:, j % RING, 0:n], raw[:, j % RING, 0:n], whi[:, j % RING, 0:n],
                                        ALU.subtract).then_inc(lo_ready, 1)

            roots = [0]

            def ask_root(dst, src, scale, eps):
                roots[0] += 1
                nc.vector.tensor_scalar(dst, src, scale, eps, ALU.mult, ALU.add).then_inc(root_asked, 1)

            def finish(sub, t):
                w = 1.0 if sub == 1 else 0.5
                buf = LAST[sub][1]
                dve.wait_ge(squared, TT * BLK * (sub + 1) - TT + t + 1)
                link(nc.vector.reduce_sum(stat[:, TMP + t:TMP + t + 1], fsq[:, t, :], AX.X))
                ask_root(stat[:, RPOST + t:RPOST + t + 1], stat[:, TMP + t:TMP + t + 1], 1.0 / D / w ** 2, EPS / w ** 2)
                if t == 0:
                    link(gain_tile(sub, buf, BLK - 1, t))
                    dve.wait_ge(acc_free[1 - buf], LEFT[sub][1 - buf])

            def last_gain(sub):
                buf = LAST[sub][1]
                gain_tile(sub, buf, BLK - 1, TT - 1).then_inc(acc_free[buf], 1)
                dve.wait_ge(acc_free[buf], LEFT[sub][buf])

            def add_tile(h, t, end):
                r = res[:, t, h * HW:end * HW].rearrange("p (h n) -> p h n", n=HW)
                return nc.vector.scalar_tensor_tensor(out=r, in0=fout[:, h:end, t, :], scalar=stat[:, RPOST + t:RPOST + t + 1],
                                                      in1=r, op0=ALU.mult, op1=ALU.add)

            def add_half(h, a=0, b=TT):
                for t in range(a, b):
                    ins = add_tile(h, t, h + 1)
                ins.then_inc(res_ready, 1)

            def act_lo_half(p, h, a=0, b=TT):
                dve.wait_ge(acthi_ready, half_count(p, h, b - 1))
                for k in range(2):
                    kt = 2 * h + k
                    ins = nc.vector.scalar_tensor_tensor(out=act_lo[:, h, a:b, k, :], in0=block_tiles(kt % NH, a, b),
                                                         scalar=vec[:, PRE[p] + kt:PRE[p] + kt + 1], in1=act_hi[:, h, a:b, k, :],
                                                         op0=ALU.mult, op1=ALU.subtract)
                ins.then_inc(actlo_ready, 1)

            def row_factor(p):
                dve.wait_ge(ssq_ready, TT * (p + 1))
                ask_root(stat[:, RSTD:RSTD + 2], stat[:, TMP:TMP + 2], 1.0 / D, EPS)
                dve.wait_ge(root_ready, roots[0])

            def start_phase(p, lo_at):
                add = add_half if p else lambda h: None
                split = lambda h, a=0, b=TT: act_lo_half(p, h, a, b)
                if p == 0:
                    for h in range(2):
                        split(h)
                        lo_at(h)
                    lo_at(2)
                    split(2)
                    lo_at(3)
                else:
                    finish(p - 1, 0)
                    dve.wait_ge(root_ready, roots[0])
                    add_tile(0, 0, 2).then_inc(res_ready, 2)
                    lo_at(0)
                    add(2, 0, 1)
                    split(0, 0, 1)
                    split(1, 0, 1)
                    lo_at(1)
                    finish(p - 1, 1)
                    split(2, 0, 1)
                    dve.wait_ge(root_ready, roots[0])
                    add_tile(0, 1, 2).then_inc(res_ready, 2)
                    lo_at(2)
                    split(0, 1, 2)
                    add(2, 1, 2)
                    split(1, 1, 2)
                    add(3)
                    split(2, 1, 2)
                    lo_at(3)
                add(4)
                split(3)
                if p:
                    last_gain(p - 1)
                lo_at(4)
                add(5)
                split(4)
                lo_at(5)
                add(6)
                split(5)
                lo_at(6)
                add(7)
                if p == 0:
                    dve.wait_ge(vec_psum, 2)
                    nc.vector.tensor_copy(vec[:, KT:KT + NVEC], acc[:, 1, 0, 0:NVEC]).then_inc(vec_ready, 1)
                split(6)
                lo_at(7)
                split(7)

            def gain_tile(sub, buf, o, t):
                dve.wait_ge(squared, TT * BLK * sub + TT * o + t + 1)
                return nc.vector.tensor_tensor(fout[:, 2 * o:2 * o + 2, t, :], acc[:, buf, t, :].rearrange("p (h n) -> p h n", n=HW),
                                               gpost[:, o * CW:(o + 1) * CW].rearrange("p (h n) -> p h n", n=HW), ALU.mult)

            def times_gain(sub, buf, o):
                for t in range(TT):
                    ins = gain_tile(sub, buf, o, t)
                ins.then_inc(acc_free[buf], 1)

            def ffn(f):
                base, p = ffn_base[f], 2 * f

                def hidden(chunk, done):
                    dve.wait_ge(mm_done, done)
                    dve.wait_ge(acc_free[0], freed0[f][0] + chunk + 1)
                    for t in range(TT):
                        ins = nc.vector.scalar_tensor_tensor(out=nat[:, t, :], in0=acc[:, 1, t, :], scalar=stat[:, RSTD + t:RSTD + t + 1],
                                                             in1=sg[:, t, :], op0=ALU.mult, op1=ALU.mult)
                    ins.then_inc(acc_free[1], 1)

                def hidden_lo(chunk):
                    dve.wait_ge(hhi_ready, UP_CHUNKS * f + chunk + 1)
                    kts = bass.ds(KB * chunk, KB)
                    nc.vector.tensor_tensor(h_lo[:, kts, :], blocks[:, 0:KB, :], h_hi[:, kts, :], ALU.subtract).then_inc(hlo_ready, 1)

                start_phase(p, lambda j: lo(j, base + j + 1))
                for j in range(8, 16):
                    lo(j, base + j + 1)
                    if j == 9:
                        row_factor(p)
                with dve.Fori(1, UP_CHUNKS) as it:
                    first = base + UP_SLABS * it
                    for j in range(16):
                        lo(j, first + j + 1)
                        if j == 3:
                            hidden(it - 1, first)
                        if j == 9:
                            hidden_lo(it - 1)
                down0 = base + UP_CHUNKS * UP_SLABS
                dve.wait_ge(gpost_full, 16 if f == 0 else 48)
                for o in range(BLK):
                    for j in range(DOWN_SLABS):
                        n = DOWN_SLABS * o + j
                        lo(n, down0 + n + 1)
                        if o == 0 and j == 3:
                            hidden(UP_CHUNKS - 1, down0)
                        if o == 0 and j == 9:
                            hidden_lo(UP_CHUNKS - 1)
                        if o and j == 4:
                            times_gain(2 * f, (o - 1) % 2, o - 1)

            def lo_in(name, j, kts=SK, width=CW):
                lo(j, MIX[name][0] + j + 1, kts, width)

            taps = [0]

            def conv(n):
                for s in range(taps[0], min(taps[0] + n, CT * TAPS)):
                    c, w = s // (2 * TAPS) * 2 + s % 2, s % (2 * TAPS) // 2
                    if s % (2 * TAPS) == 0:
                        dve.wait_ge(tr_evicted, 3 if c < KB else 6)
                    src, dst = conv_in[:, c, w:w + SEQ], conv_out[:, c, :]
                    if w == 0:
                        ins = nc.vector.tensor_scalar(dst, src, dwt[:, c, 0:1], vec[:, DWB + c:DWB + c + 1], ALU.mult, ALU.add)
                    else:
                        dve.wait_ge(conv_tap, s - 1)
                        ins = nc.vector.scalar_tensor_tensor(out=dst, in0=src, scalar=dwt[:, c, w:w + 1], in1=dst,
                                                             op0=ALU.mult, op1=ALU.add)
                    ins.then_inc(conv_tap, 1)
                taps[0] = min(taps[0] + n, CT * TAPS)

            def produced(name):
                n0, slabs, buf, _ = MIX[name]
                dve.wait_ge(mm_done, n0 + slabs)
                return buf

            def glu_scale(i):
                buf = produced(f"a{i}")
                if i:
                    dve.wait_ge(tr_psum, 3)
                for t in range(TT):
                    ins = nc.vector.tensor_scalar(nat[:, t, :], acc[:, buf, t, :], stat[:, RSTD + t:RSTD + t + 1], None, ALU.mult)
                ins.then_inc(acc_free[buf], 1)

            def glu_mult(i):
                for name in f"gt{i}", f"a{i}":
                    _, _, buf, freed = MIX[name]
                    dve.wait_ge(acc_free[buf], freed + 1)
                nc.vector.tensor_tensor(nat[:], nat[:], sg[:], ALU.mult).then_inc(glu_ready, 1)

            def gate_bias(name, g, dst):
                buf = produced(name)
                dve.wait_ge(bgate_full[g % 2], 16 * (g // 2 + 1))
                for t in range(TT):
                    ins = nc.vector.scalar_tensor_tensor(out=dst[:, t, :], in0=acc[:, buf, t, :], scalar=stat[:, RSTD + t:RSTD + t + 1],
                                                         in1=bgate[:, g % 2, :], op0=ALU.mult, op1=ALU.add)
                ins.then_inc(acc_free[buf], 1)

            def add_scores(u):
                t, n, at0 = (1, SEQ, 0) if u % 2 == 0 else (0, P, SEQ)
                dve.wait_ge(relu_ready, u + 1)
                for a, dst in ((0, score), (1, work)):
                    d, h = dst[:, at0:at0 + n], u // 2 * 2 + a
                    src, w = relu_d[:, u % 2, a * n:(a + 1) * n], small[:, t, IDIM + h:IDIM + h + 1]
                    if u < 2:
                        ins = nc.vector.tensor_scalar(d, src, w, None, ALU.mult)
                    else:
                        dve.wait_ge(score_added, 2 * (u - 2) + a + 1)
                        ins = nc.vector.scalar_tensor_tensor(out=d, in0=src, scalar=w, in1=d, op0=ALU.mult, op1=ALU.add)
                    ins.then_inc(score_added, 1)

            def top8(r):
                parts = ((0, 0, SEQ), (1, SEQ, P))
                src = score if r == 0 else work
                for i, a, n in parts:
                    ins = nc.vector.max(stat[:, MAX8 + 8 * i:MAX8 + 8 * i + 8], src[:, a:a + n])
                link(ins)
                for i, a, n in parts:
                    ins = nc.vector.match_replace(work[:, a:a + n], stat[:, MAX8 + 8 * i:MAX8 + 8 * i + 8], src[:, a:a + n], TAKEN)
                link(ins)

            def attend(k):
                if 0 <= k - 1 < HEADS:
                    lg, s = logit[(k - 1) % 2], (k - 1) % 2 * 2
                    dve.wait_ge(exp_ready, k)
                    link(nc.vector.reciprocal(stat[:, RINV + s:RINV + s + 2], stat[:, RSUM + s:RSUM + s + 2]))
                    nc.vector.tensor_scalar(lg[:, 0:SEQ], lg[:, 0:SEQ], stat[:, RINV + s:RINV + s + 1], None, ALU.mult)
                    nc.vector.tensor_scalar(lg[:, SEQ:SPAN], lg[:, SEQ:SPAN], stat[:, RINV + s + 1:RINV + s + 2], None,
                                            ALU.mult).then_inc(prob_ready, 1)
                if 0 <= k - 3 < HEADS:
                    h = k - 3
                    dve.wait_ge(athi_ready, h + 1)
                    nc.vector.tensor_tensor(attn_lo[:, h, :], msc[:, 3, SEQ * (h % 2):SEQ * (h % 2) + SEQ], attn_hi[:, h, :],
                                            ALU.subtract).then_inc(atlo_ready, 1)
                if k < HEADS:
                    lg, s = logit[k % 2], k % 2 * 2
                    dve.wait_ge(logit_psum, k + 1)
                    if k >= 2:
                        dve.wait_ge(pt_psum, k - 1)
                    link(nc.vector.scalar_tensor_tensor(out=lg[:], in0=msc[:, k % 2, 0:SPAN], scalar=float(HD) ** -0.5,
                                                        in1=bias[:, k, :], op0=ALU.mult, op1=ALU.add))
                    for i, a, n in ((0, 0, SEQ), (1, SEQ, P)):
                        ins = nc.vector.tensor_tensor_reduce(out=lg[:, a:a + n], in0=lg[:, a:a + n], in1=addmask[:, a:a + n],
                                                             scale=1.0, scalar=2 * TAKEN, op0=ALU.add, op1=ALU.max,
                                                             accum_out=stat[:, MX + s + i:MX + s + i + 1])
                    link(ins)
                    nc.vector.tensor_scalar(stat[:, NMX + s:NMX + s + 2], stat[:, MX + s:MX + s + 2], -1.0, None,
                                            ALU.mult).then_inc(max_ready, 1)

            dve.wait_ge(vec_psum, 1)
            nc.vector.tensor_copy(vec[:, 0:KT], acc[:, 1, 0, 0:KT]).then_inc(vec_ready, 1)
            dve.wait_ge(vec_ready, 1)
            ffn(0)
            start_phase(1, lambda j: lo_in("a0", j))
            for j in range(8):
                lo_in("gt0", j)
                if j == 1:
                    row_factor(1)
                if j == 4:
                    glu_scale(0)
            for j in range(4):
                lo_in("kiwi", j, 4, NSMALL)
            for j in range(8):
                lo_in("a1", j)
                if j == 1:
                    glu_mult(0)
            for j in range(8):
                lo_in("gt1", j)
                if j == 4:
                    glu_scale(1)
                if j > 5:
                    conv(4)
            for j in range(8):
                lo_in("qk0", j)
                if j == 5:
                    glu_mult(1)
                conv(4)
            dve.wait_ge(tr_evicted, 4)
            link(nc.vector.tensor_scalar(small[:, :, IDIM:NSMALL], small[:, :, IDIM:NSMALL], float(IH) ** -0.5, None, ALU.mult))
            for name in [f"qk{i}" for i in range(1, 6)] + ["v0", "v1"]:
                for j in range(8):
                    lo_in(name, j)
                    conv(4)
            conv(CT * TAPS)
            for j in range(8):
                lo_in("gc0", j)
                if j >= 6:
                    add_scores(j - 6)
            for j in range(8):
                lo_in("gc1", j)
                if j == 1:
                    dve.wait_ge(ln_psum, 1)
                    mu = msc[:, 0:1, 0:SEQ].to_broadcast([P, CT, SEQ])
                    nc.vector.tensor_tensor(conv_out[:], conv_out[:], mu, ALU.subtract).then_inc(ln_centred, 1)
                add_scores(2 + j)
                if j == 4:
                    gate_bias("gc0", 0, gconv[:, 0])
            for j in range(8):
                lo_in("gc2", j)
                if j == 0:
                    dve.wait_ge(ln_psum, 2)
                    nc.vector.tensor_scalar(ln_rstd[:, 0, :], msc[:, 1, 0:SEQ], EPS, None, ALU.add).then_inc(ln_var, 1)
                if j == 3:
                    dve.wait_ge(ln_std, 1)
                    link(nc.vector.reciprocal(ln_rstd[:], ln_rstd[:]))
                    nc.vector.tensor_tensor(conv_out[:], conv_out[:], ln_rstd[:].to_broadcast([P, CT, SEQ]),
                                            ALU.mult).then_inc(ln_scaled, 1)
                if j < 6:
                    add_scores(10 + j)
                if j == 5:
                    gate_bias("gc1", 1, gconv[:, 1])
                if j == 6:
                    dve.wait_ge(score_added, 2 * IH)
                    nc.vector.tensor_tensor(score[:], score[:], work[:], ALU.add).then_inc(score_added, 1)
            dve.wait_ge(score_masked, 1)
            for j in range(8):
                lo_in("gc3", j)
                top8(j)
                if j == 0:
                    dve.wait_ge(convhi_ready, 1)
                    nc.vector.tensor_tensor(conv_lo[:], conv_out[:], conv_hi[:], ALU.subtract).then_inc(convlo_ready, 1)
                if j == 4:
                    gate_bias("gc2", 2, gconv[:, 2])
            link(nc.vector.tensor_tensor(addmask[:], work[:], score[:], ALU.is_equal))
            nc.vector.tensor_scalar(addmask[:], addmask[:], MASKED, None, ALU.mult).then_inc(sel_ready, 1)
            dve.wait_ge(bias_full, 32 * HEADS)

            def gate_conv(i):
                buf = produced(f"pw{i}")
                dve.wait_ge(gate_ready, i + 1)
                nc.vector.tensor_tensor(gconv[:, i], gconv[:, i], acc[:, buf], ALU.mult).then_inc(acc_free[buf], 1)

            for g in range(24):
                lo_in(f"pw{g // 4}" if g < 16 else "ga0", g % 4 if g < 16 else g - 16)
                if g == 3:
                    gate_bias("gc3", 3, gconv[:, 3])
                    dve.wait_ge(mask_ready, 1)
                if g % 4 == 3 and 7 <= g < 20:
                    gate_conv(g // 4 - 1)
                if g % 2 == 1 and g >= 3:
                    attend((g - 3) // 2)
            for i in range(BLK):
                for j in range(4):
                    lo_in(f"wo{i}", j)
                gate_bias(f"ga{i}", BLK + i, sg)
                nxt = f"ga{i + 1}" if i < BLK - 1 else "out0"
                for j in range(8):
                    lo_in(nxt, j)
                    if j == 3:
                        buf = produced(f"wo{i}")
                        dve.wait_ge(gate_ready, BLK + i + 1)
                        nc.vector.tensor_tensor(sg[:], sg[:], acc[:, buf], ALU.mult).then_inc(acc_free[buf], 1)
                        dve.wait_ge(acc_free[buf], MIX[f"wo{i}"][3] + 1)
                        if i:
                            dve.wait_ge(mixed_psum, i)
                        nc.vector.tensor_tensor(nat[:], sg[:], gconv[:, i], ALU.add).then_inc(mixed_ready, 1)
                    if j == 7:
                        dve.wait_ge(mixhi_ready, i + 1)
                        nc.vector.tensor_tensor(mix_lo[:, KB * i:KB * i + KB, :], blocks[:, KB * (i % 2):KB * (i % 2) + KB, :],
                                                mix_hi[:, KB * i:KB * i + KB, :], ALU.subtract).then_inc(mixlo_ready, 1)
            dve.wait_ge(gpost_full, 32)
            for i in range(1, BLK):
                for j in range(8):
                    lo_in(f"out{i}", j)
                    if j == 3:
                        times_gain(1, MIX[f"out{i - 1}"][2], i - 1)
            ffn(1)
            for t in range(TT):
                finish(2, t)
                if t:
                    last_gain(2)
                dve.wait_ge(root_ready, roots[0])
                for a, b in LAST_ADDS if t else [(h, h + 1) for h in range(NH)]:
                    add_tile(a, t, b).then_inc(res_ready, 1)

        @block.tensor
        def _(pe):
            def mm(o, a, b, **kw):
                return nc.tensor.matmul(o, a, b, **kw)

            def slab_tile(t, j, ready, buf, hi_, lo_, first, last, kts=SK, width=CW):
                pe.wait_ge(lo_ready, ready)
                vh, vl = slot_view(whi, j % RING, kts, width), slot_view(wlo, j % RING, kts, width)
                for k in range(kts):
                    kt = first + k
                    o = acc[:, buf, t, 0:width]
                    mm(o, k_tile(hi_, kt, t), vh[:, k, :], start=kt == 0, stop=False)
                    mm(o, k_tile(hi_, kt, t), vl[:, k, :], start=False, stop=False)
                    ins = mm(o, k_tile(lo_, kt, t), vh[:, k, :], start=False, stop=kt == last)
                return ins

            def slab(*args, **kw):
                for t in range(TT):
                    ins = slab_tile(t, *args, **kw)
                ins.then_inc(mm_done, 1)

            def last_slabs(p, args_of):
                for j in range(RING):
                    ins = slab_tile(0, *args_of(j))
                ins.then_inc(tile0_done, 1)
                for j in range(RING):
                    slab_tile(1, *args_of(j)).then_inc(mm_done, 1)
                    if j == 1 and p < 3:
                        act_half(p, 0, 0, 1)
                        act_half(p, 1, 0, 1)

            def transposed(src, block0, tiles, a=0, b=TT):
                for k in range(tiles):
                    for t in range(a, b):
                        ins = nc.tensor.transpose(blocks[:, block0 + k, t * P:(t + 1) * P], src[:, t, k * P:(k + 1) * P], ident[:])
                return ins

            def act_half(p, h, a=0, b=TT):
                if p == 0:
                    pe.wait_ge(x_full[h // 2], 16)
                else:
                    pe.wait_ge(res_ready, res_count(p, h, b - 1))
                if h >= BLK:
                    pe.wait_ge(actlo_ready, half_count(p, h - BLK))
                elif a:
                    pe.wait_ge(actlo_ready, half_count(p, h, 0))
                transposed(res[:, :, h * HW:(h + 1) * HW], 2 * h % NH, 2, a, b).then_inc(act_psum, 1)

            def start_phase(p, args_of):
                if p == 0:
                    act_half(p, 0)
                    act_half(p, 1)
                    for j in range(TILED):
                        pe.wait_ge(actlo_ready, half_count(p, j))
                        slab(*args_of(j))
                        act_half(p, j + 2)
                else:
                    act_half(p, 2, 0, 1)
                    for j in range(TILED):
                        if j == TILED - 1:
                            act_half(p, 0, 1, 2)
                            act_half(p, 1, 1, 2)
                        pe.wait_ge(actlo_ready, half_count(p, j, 0))
                        slab_tile(0, *args_of(j))
                    act_half(p, 2, 1, 2)
                    for j in range(TILED):
                        pe.wait_ge(actlo_ready, half_count(p, j, 1))
                        slab_tile(1, *args_of(j)).then_inc(mm_done, 1)
                        if j < 2:
                            act_half(p, 3 + j)
                for j in range(TILED, NH):
                    pe.wait_ge(actlo_ready, half_count(p, j))
                    slab(*args_of(j))
                    if j < 6:
                        act_half(p, j + 2)
                    if j == 4 and p == 0:
                        pe.wait_ge(vec_loaded, 16 * 5)
                        nc.tensor.transpose(acc[:, 1, 0, 0:NVEC], vrows[0:NVEC, :], ident[0:NVEC, 0:NVEC]).then_inc(vec_psum, 1)

            def ffn(f):
                base, p = ffn_base[f], 2 * f

                def up(it, peeled):
                    def args_of(j):
                        return j, base + UP_SLABS * it + j + 1, j // 8, act_hi, act_lo, (j % 8) * SK, KT - 1

                    for m in range(2):
                        if peeled and f == 0 and m == 1:
                            pe.wait_ge(vec_ready, 2)
                        if not (peeled and f == 0):
                            pe.wait_ge(acc_free[m], freed0[f][m] + it)
                        if peeled and m == 0:
                            start_phase(p, args_of)
                            continue
                        for j in range(8 * m, 8 * m + 8):
                            slab(*args_of(j))
                            if j == 4 and not peeled:
                                hidden_transpose(it - 1)

                def hidden_transpose(chunk):
                    pe.wait_ge(acc_free[1], freed0[f][1] + chunk + 1)
                    transposed(nat[:], 0, KB).then_inc(h_psum, 1)

                up(0, True)
                with pe.Fori(1, UP_CHUNKS) as it:
                    up(it, False)
                down0 = base + UP_CHUNKS * UP_SLABS
                for o in range(BLK):
                    pe.wait_ge(acc_free[o % 2], freed0[f][o % 2] + UP_CHUNKS + o // 2)
                    def args_of(j):
                        n = DOWN_SLABS * o + j
                        return n, down0 + n + 1, o % 2, h_hi, h_lo, j * SK, FT - 1

                    for j in range(DOWN_SLABS - (RING if o == BLK - 1 else 0)):
                        if o == 0 and j == DOWN_SLABS - KB // SK:
                            pe.wait_ge(hlo_ready, UP_CHUNKS * (f + 1))
                        slab(*args_of(j))
                        if o == 0 and j == 4:
                            hidden_transpose(UP_CHUNKS - 1)
                last_slabs(p + 1, lambda j: args_of(DOWN_SLABS - RING + j))

            def slabs(name, a, b, hi_=act_hi, lo_=act_lo, kts=SK, width=CW):
                n0, count, buf, freed = MIX[name]
                if a == 0:
                    pe.wait_ge(acc_free[buf], freed)

                def args_of(j):
                    return j, n0 + j + 1, buf, hi_, lo_, j * kts, count * kts - 1, kts, width

                ahead = RING if name == f"out{BLK - 1}" else 0
                for j in range(a, b - ahead):
                    slab(*args_of(j))
                if ahead:
                    last_slabs(2, lambda j: args_of(count - RING + j))

            def tr(i, emit):
                if i >= 2:
                    pe.wait_ge(tr_evicted, i - 1)
                emit(KB * (i % 2)).then_inc(tr_psum, 1)

            def tr_nat(i):
                tr(i, lambda b0: transposed(nat[:], b0, KB))

            def tr_dw(b0):
                for c in range(CT):
                    ins = nc.tensor.transpose(msc[:, 0, c * TAPS:(c + 1) * TAPS], dw_rows[:, c * P:(c + 1) * P], ident[0:TAPS, 0:TAPS])
                return ins

            def tr_rel(b0):
                return mm(msc[0:HEADS, 2, 0:RELS], relb[:], onehot[:, 0:RELS], start=True, stop=True)

            def tr_small(b0):
                for t in range(TT):
                    ins = nc.tensor.transpose(blocks[:, b0, t * P:t * P + NSMALL], small_t[:, t * P:(t + 1) * P],
                                              ident[0:NSMALL, 0:NSMALL])
                return ins

            def tr_ki(b0):
                pe.wait_ge(tr_evicted, 4)
                for a in range(2):
                    for t in range(TT):
                        ins = nc.tensor.transpose(blocks[:, b0 + a, t * P:(t + 1) * P], ki_pad[:, t, a, :], ident[:])
                return ins

            def dots(u):
                t, n = (1, SEQ) if u % 2 == 0 else (0, P)
                if u >= 2:
                    pe.wait_ge(relu_ready, u - 1)
                mm(msc[:, 2 + u % 2, 0:2 * n], qi_t[:, u // 2, t * P:(t + 1) * P], ki_t[:, :, 0:n],
                   start=True, stop=True).then_inc(dots_ready, 1)

            def channel_mean(bank, src):
                for c in range(CT):
                    ins = mm(msc[:, bank, 0:SEQ], mean_w[:], src[:, c, :], start=c == 0, stop=c == CT - 1)
                ins.then_inc(ln_psum, 1)

            def attend(k):
                if k < HEADS:
                    if k >= 2:
                        pe.wait_ge(max_ready, k - 1)
                    o = msc[:, k % 2, :]
                    mm(o[:, 0:SEQ], q_t[:, k, P:SEQ], k_t[:, k, :], start=True, stop=True)
                    mm(o[:, SEQ:SPAN], q_t[:, k, 0:P], k_t[:, k, 0:P], start=True, stop=True).then_inc(logit_psum, 1)
                if 0 <= k - 2 < HEADS:
                    h, lg = k - 2, logit[k % 2]
                    pe.wait_ge(prob_ready, h + 1)
                    if h:
                        pe.wait_ge(pt_ready, h)
                    nc.tensor.transpose(msc[:, 2, 0:P], lg[:, SEQ:SPAN], ident[:])
                    nc.tensor.transpose(msc[:, 2, P:SEQ], lg[:, 0:P], ident[:])
                    nc.tensor.transpose(msc[:, 2, SEQ:SPAN], lg[:, P:SEQ], ident[:]).then_inc(pt_psum, 1)
                if 0 <= k - 3 < HEADS:
                    h = k - 3
                    pe.wait_ge(pt_ready, h + 1)
                    if h:
                        pe.wait_ge(atlo_ready, h)
                    o = msc[:, 3, SEQ * (h % 2):SEQ * (h % 2) + SEQ]
                    mm(o, v_n[:, 0, h * HD:(h + 1) * HD], p_t[:, h % 2, 0:SEQ], start=True, stop=False)
                    mm(o[:, P:SEQ], v_n[:, 1, h * HD:(h + 1) * HD], p_t[:, h % 2, SEQ:SPAN], start=False,
                       stop=True).then_inc(pv_psum, 1)

            pe.wait_ge(consts_ready, 1)
            pe.wait_ge(first_loaded, 16)
            nc.tensor.transpose(acc[:, 1, 0, 0:KT], vfirst[:], ident[0:KT, 0:KT]).then_inc(vec_psum, 1)
            ffn(0)
            pe.wait_ge(acc_free[0], MIX["a0"][3])
            start_phase(1, lambda j: (j, MIX["a0"][0] + j + 1, 0, act_hi, act_lo, j * SK, KT - 1))
            slabs("gt0", 0, 5)
            pe.wait_ge(mixrows_full, 48)
            tr(0, tr_dw)
            tr(1, tr_rel)
            slabs("gt0", 5, 8)
            n0 = MIX["kiwi"][0]
            for j in range(4):
                pe.wait_ge(lo_ready, n0 + j + 1)
                vh, vl = slot_view(whi, j, 4, NSMALL), slot_view(wlo, j, 4, NSMALL)
                for k in range(4):
                    kt, o = 4 * j + k, kiwi.rearrange("m (t n) -> m t n", n=P)
                    th, tl = act_hi[:, kt // 2, :, kt % 2, :], act_lo[:, kt // 2, :, kt % 2, :]
                    mm(o, vh[:, k, :], th, start=kt == 0, stop=False)
                    mm(o, vh[:, k, :], tl, start=False, stop=False)
                    ins = mm(o, vl[:, k, :], th, start=False, stop=kt == KT - 1)
                ins.then_inc(mm_done, 1)
            slabs("a1", 0, 3)
            pe.wait_ge(glu_ready, 1)
            pe.wait_ge(kiwi_evicted, 1)
            tr_nat(2)
            slabs("a1", 3, 5)
            tr(3, tr_small)
            slabs("a1", 5, 8)
            slabs("gt1", 0, 5)
            tr(4, tr_ki)
            slabs("gt1", 5, 8)
            slabs("qk0", 0, 7)
            pe.wait_ge(glu_ready, 2)
            tr_nat(5)
            slabs("qk0", 7, 8)
            names = [f"qk{i}" for i in range(6)] + ["v0", "v1"]
            for i in range(6):
                slabs(names[i + 1], 0, 5)
                pe.wait_ge(acc_free[MIX[names[i]][2]], MIX[names[i]][3] + 1)
                tr_nat(6 + i)
                slabs(names[i + 1], 5, 8)
            slabs("v1", 0, 8)
            for j in range(8):
                slabs("gc0", j, j + 1)
                if j == 5:
                    pe.wait_ge(conv_tap, CT * TAPS)
                    channel_mean(0, conv_out)
                if j >= 2:
                    dots(j - 2)
            for j in range(8):
                slabs("gc1", j, j + 1)
                dots(6 + j)
                if j == 4:
                    pe.wait_ge(ln_squares, 1)
                    channel_mean(1, squares)
            slabs("gc2", 0, 1)
            dots(14)
            slabs("gc2", 1, 2)
            dots(15)
            slabs("gc2", 2, 8)
            slabs("gc3", 0, 8)
            attend(0)
            pe.wait_ge(convlo_ready, 1)
            for g in range(24):
                if g < 16:
                    slabs(f"pw{g // 4}", g % 4, g % 4 + 1, conv_hi, conv_lo)
                else:
                    slabs("ga0", g - 16, g - 15)
                if g % 2 == 1 and g < 20:
                    attend((g + 1) // 2)
            pe.wait_ge(atlo_ready, HEADS)
            for i in range(BLK):
                slabs(f"wo{i}", 0, 4, attn_hi, attn_lo)
                for j in range(8):
                    if i < BLK - 1:
                        slabs(f"ga{i + 1}", j, j + 1)
                    else:
                        if j == 6:
                            pe.wait_ge(mixlo_ready, BLK)
                        slabs("out0", j, j + 1, mix_hi, mix_lo)
                    if j == 3:
                        pe.wait_ge(mixed_ready, i + 1)
                        if i >= 2:
                            pe.wait_ge(mixlo_ready, i - 1)
                        transposed(nat[:], KB * (i % 2), KB).then_inc(mixed_psum, 1)
            for i in range(1, BLK):
                slabs(f"out{i}", 0, 8, mix_hi, mix_lo)
            ffn(1)


_INS = ["x", "rel_bias", "ffn1_pre_g", "ffn1_wg", "ffn1_wu", "ffn1_wd", "ffn1_post_g", "mix_pre_g", "w_in",
        "b_gate", "w_o", "conv_dw", "conv_dw_b", "conv_ln_g", "conv_ln_b", "w_pw2", "w_out", "mix_post_g",
        "ffn2_pre_g", "ffn2_wg", "ffn2_wu", "ffn2_wd", "ffn2_post_g"]


def bucket_rows():
    n = np.maximum(2 * P - 1 - np.arange(RELS), 0)
    exact = BUCKETS // 2
    big = exact + (np.log(np.maximum(n, exact).astype(np.float32) / np.float32(exact)) / np.float32(np.log(P / exact))
                   * np.float32(BUCKETS - exact)).astype(np.int32)
    b = np.where(n < exact, n, np.minimum(big, BUCKETS - 1))
    return (np.arange(BUCKETS)[:, None] == b[None, :]).astype(np.float32)


def kernel(**inputs):
    import concourse.bacc as _bacc
    from concourse.bass_utils import run_bass_kernel_spmd as _run

    nc = _bacc.Bacc("TRN2", target_bir_lowering=False, num_devices=1)
    arrays, args = {}, []
    for name in _INS:
        a = np.ascontiguousarray(inputs[name])
        arrays[f"in_{name}_dram"] = a
        ap = nc.dram_tensor(f"in_{name}_dram", a.shape, mybir.dt.from_np(a.dtype), kind="ExternalInput").ap()
        args.append(ap if name == "rel_bias" else ap[0])
    arrays["in_bucket_rows_dram"] = bucket_rows()
    args.append(nc.dram_tensor("in_bucket_rows_dram", (BUCKETS, RELS), mybir.dt.float32, kind="ExternalInput").ap())
    args.append(nc.dram_tensor("bias_scratch", (HEADS, P, RELS), mybir.dt.float32).ap())
    o = nc.dram_tensor("out_0_dram", (1, SEQ, D), mybir.dt.float32, kind="ExternalOutput").ap()
    build(nc, *args, o[0])
    r = _run(nc, [arrays], core_ids=[0])
    return r.results[0]["out_0_dram"]
```
